# Optimizing a Trainium2 kernel written in Bass

```python
import math
import jax, jax.numpy as jnp
from jax import lax
import numpy as np

D_MODEL = 1024
BATCH = 1
SEQ = 256
DEPTH = 2

N_A = DEPTH // 2
N_B = DEPTH - N_A
N_DENSE = (DEPTH + 1) // 2
N_MOE = DEPTH // 2

LA_HEADS = 8
LA_DK = 128
LA_DV = 128
QK_W = LA_HEADS * LA_DK
V_W = LA_HEADS * LA_DV
QKV_W = 2 * QK_W + V_W
A_PROJ_W = QKV_W + V_W + 2 * LA_HEADS
CONV_W = 4
CHUNK = 64

SW_HEADS = 16
SW_KV_HEADS = 4
SW_GROUP = SW_HEADS // SW_KV_HEADS
SW_HD = 64
Q_W = SW_HEADS * SW_HD
KV_W = SW_KV_HEADS * SW_HD
WINDOW = 128
BLOCK = 128

N_BUCKETS = 32
MAX_DIST = 128

D_FF = 3584
N_EXPERTS = 8
TOP_K = 2

EPS = 1e-6
NEG_INF = -1e30

kernel_name = "yoco_gdn_swa_sink_moe"

def rms_norm(x, g):
    xf = x.astype(jnp.float32)
    y = xf * lax.rsqrt(jnp.mean(xf * xf, axis=-1, keepdims=True) + EPS)
    return (y * g.astype(jnp.float32)).astype(x.dtype)

def l2_norm(x):
    return x * lax.rsqrt(jnp.sum(x * x, axis=-1, keepdims=True) + EPS)

def causal_depthwise_conv(x, w):
    c = x.shape[-1]
    return lax.conv_general_dilated(
        x, w[:, None, :].astype(x.dtype), window_strides=(1,),
        padding=[(CONV_W - 1, 0)], dimension_numbers=('NWC', 'WIO', 'NWC'),
        feature_group_count=c)

def chunk_gated_delta_rule(q, k, v, g, beta):
    f32 = jnp.float32
    b_, s_, h_, dk = q.shape
    dv = v.shape[-1]
    n = s_ // CHUNK

    def chunks(t):
        t = t.astype(f32).reshape((b_, n, CHUNK, h_) + t.shape[3:])
        return jnp.moveaxis(t, 3, 1)

    q = chunks(q) * (dk ** -0.5)
    k = chunks(k)
    v = chunks(v)
    beta = chunks(beta)
    g = jnp.cumsum(chunks(g), axis=-1)
    k_beta = k * beta[..., None]
    v_beta = v * beta[..., None]

    idx = np.arange(CHUNK)
    lower_incl = idx[:, None] >= idx[None, :]
    strict = idx[:, None] > idx[None, :]
    diff = g[..., :, None] - g[..., None, :]
    decay = jnp.where(lower_incl, jnp.exp(jnp.where(lower_incl, diff, 0.0)), 0.0)

    a = jnp.einsum('bhncd,bhnsd->bhncs', k_beta, k) * decay
    a = jnp.where(strict, a, 0.0) + jnp.eye(CHUNK, dtype=f32)
    rhs = jnp.concatenate([v_beta, k_beta * jnp.exp(g)[..., None]], axis=-1)
    sol = lax.linalg.triangular_solve(a, rhs, left_side=True, lower=True, unit_diagonal=True)
    u, w = sol[..., :dv], sol[..., dv:]

    attn_intra = jnp.einsum('bhncd,bhnsd->bhncs', q, k) * decay
    qe = q * jnp.exp(g)[..., None]
    g_last = g[..., -1]
    k_tail = k * jnp.exp(g_last[..., None] - g)[..., None]

    def step(state, inp):
        qe_i, w_i, u_i, a_i, k_i, gl_i = inp
        v_new = u_i - jnp.einsum('bhck,bhkv->bhcv', w_i, state)
        o = jnp.einsum('bhck,bhkv->bhcv', qe_i, state) + jnp.einsum('bhcs,bhsv->bhcv', a_i, v_new)
        state = state * jnp.exp(gl_i)[..., None, None] + jnp.einsum('bhck,bhcv->bhkv', k_i, v_new)
        return state, o

    xs = tuple(jnp.moveaxis(t, 2, 0) for t in (qe, w, u, attn_intra, k_tail, g_last))
    s0 = jnp.zeros((b_, h_, dk, dv), f32)
    _, o = lax.scan(step, s0, xs)
    return jnp.transpose(o, (1, 0, 3, 2, 4)).reshape(b_, s_, h_, dv)

def gated_deltanet(h, w_in, conv_w, a_log, dt_bias, g_onorm, w_out):
    b_, s_, _ = h.shape
    proj = h @ w_in
    qkv = jax.nn.silu(causal_depthwise_conv(proj[..., :QKV_W], conv_w))
    z = proj[..., QKV_W:QKV_W + V_W].reshape(b_, s_, LA_HEADS, LA_DV)
    b_in = proj[..., QKV_W + V_W:QKV_W + V_W + LA_HEADS].astype(jnp.float32)
    a_in = proj[..., QKV_W + V_W + LA_HEADS:].astype(jnp.float32)
    q = l2_norm(qkv[..., :QK_W].reshape(b_, s_, LA_HEADS, LA_DK).astype(jnp.float32))
    k = l2_norm(qkv[..., QK_W:2 * QK_W].reshape(b_, s_, LA_HEADS, LA_DK).astype(jnp.float32))
    v = qkv[..., 2 * QK_W:].reshape(b_, s_, LA_HEADS, LA_DV)
    beta = jax.nn.sigmoid(b_in)
    g = -jnp.exp(a_log.astype(jnp.float32)) * jax.nn.softplus(a_in + dt_bias.astype(jnp.float32))
    o = chunk_gated_delta_rule(q, k, v, g, beta)
    o = rms_norm(o, g_onorm) * jax.nn.silu(z.astype(jnp.float32))
    return o.reshape(b_, s_, V_W).astype(h.dtype) @ w_out

def shared_kv(h, g_kv, w_kv, g_knorm):
    b_, s_, _ = h.shape
    kv = rms_norm(h, g_kv) @ w_kv
    k = rms_norm(kv[..., :KV_W].reshape(b_, s_, SW_KV_HEADS, SW_HD), g_knorm)
    v = kv[..., KV_W:].reshape(b_, s_, SW_KV_HEADS, SW_HD)
    return k, v

def t5_bucket_np(dist):
    max_exact = N_BUCKETS // 2
    n = np.maximum(dist, 0)
    safe = np.maximum(n, 1).astype(np.float32)
    large = max_exact + (np.log(safe / max_exact) / np.log(MAX_DIST / max_exact)
                         * (N_BUCKETS - max_exact)).astype(np.int32)
    large = np.minimum(large, N_BUCKETS - 1)
    return np.where(n < max_exact, n, large).astype(np.int32)

def sliding_window_attention(h, k, v, w_q, g_qnorm, sinks, rel_bias, w_o):
    f32 = jnp.float32
    b_, s_, _ = h.shape
    nb = s_ // BLOCK
    q = rms_norm((h @ w_q).reshape(b_, s_, SW_KV_HEADS, SW_GROUP, SW_HD), g_qnorm)
    qb = q.reshape(b_, nb, BLOCK, SW_KV_HEADS, SW_GROUP, SW_HD)

    def band(t):
        tb = t.reshape(b_, nb, BLOCK, SW_KV_HEADS, SW_HD)
        prev = jnp.pad(tb[:, :-1], ((0, 0), (1, 0), (0, 0), (0, 0), (0, 0)))
        return jnp.concatenate([prev, tb], axis=2)

    kb, vb = band(k), band(v)
    scores = jnp.einsum('bnqhgd,bnkhd->bhgnqk', qb, kb).astype(f32) * (SW_HD ** -0.5)

    qi = np.arange(BLOCK)[:, None] + BLOCK
    kj = np.arange(2 * BLOCK)[None, :]
    dist = qi - kj
    band_ok = (dist >= 0) & (dist < WINDOW)
    key_pos = np.arange(nb)[:, None, None] * BLOCK - BLOCK + kj[None]
    mask = band_ok[None] & (key_pos >= 0)
    bias = rel_bias.astype(f32)[t5_bucket_np(dist)]
    bias = jnp.transpose(bias, (2, 0, 1)).reshape(SW_KV_HEADS, SW_GROUP, 1, BLOCK, 2 * BLOCK)
    scores = jnp.where(mask, scores + bias, NEG_INF)

    sink = sinks.astype(f32).reshape(SW_KV_HEADS, SW_GROUP, 1, 1, 1)
    m = jnp.maximum(jnp.max(scores, axis=-1, keepdims=True), sink)
    p = jnp.exp(scores - m)
    denom = jnp.sum(p, axis=-1, keepdims=True) + jnp.exp(sink - m)
    out = jnp.einsum('bhgnqk,bnkhd->bnqhgd', p / denom, vb.astype(f32))
    return out.reshape(b_, s_, Q_W).astype(h.dtype) @ w_o

def swiglu(h, w_gate, w_up, w_down):
    return (jax.nn.silu(h @ w_gate) * (h @ w_up)) @ w_down

def moe_swiglu(h, w_router, w_gate, w_up, w_down):
    logits = (h @ w_router).astype(jnp.float32)
    top_vals, top_idx = lax.top_k(logits, TOP_K)
    top_w = jax.nn.softmax(top_vals, axis=-1)
    gates = jnp.sum(jax.nn.one_hot(top_idx, N_EXPERTS, dtype=jnp.float32) * top_w[..., None], axis=-2)
    gates = gates.astype(h.dtype)
    y = jnp.zeros_like(h)
    for e in range(N_EXPERTS):
        y = y + gates[..., e:e + 1] * swiglu(h, w_gate[e], w_up[e], w_down[e])
    return y

def setup_inputs(seed: int = 0) -> dict:
    key = jax.random.key(seed)
    ks = iter(jax.random.split(key, 32))
    D = D_MODEL

    def nrm(shape, scale):
        return jax.random.normal(next(ks), shape, jnp.float32) * scale

    def gain(shape):
        return 1.0 + nrm(shape, 0.02)

    x = nrm((BATCH, SEQ, D), 1.0)
    a_norm = gain((N_A, D))
    a_w_in = nrm((N_A, D, A_PROJ_W), D ** -0.5)
    a_conv = nrm((N_A, CONV_W, QKV_W), CONV_W ** -0.5)
    a_log_decay = jnp.log(jax.random.uniform(next(ks), (N_A, LA_HEADS), jnp.float32, 1.0, 16.0))
    dt = jnp.exp(jax.random.uniform(next(ks), (N_A, LA_HEADS), jnp.float32,
                                    math.log(1e-3), math.log(1e-1)))
    a_dt_bias = dt + jnp.log(-jnp.expm1(-dt))
    a_out_norm = gain((N_A, LA_DV))
    a_w_out = nrm((N_A, V_W, D), V_W ** -0.5)
    kv_norm = gain((D,))
    kv_w = nrm((D, 2 * KV_W), D ** -0.5)
    k_norm = gain((SW_HD,))
    b_norm = gain((N_B, D))
    b_w_q = nrm((N_B, D, Q_W), D ** -0.5)
    q_norm = gain((N_B, SW_HD))
    b_sinks = nrm((N_B, SW_HEADS), 1.0)
    b_w_o = nrm((N_B, Q_W, D), Q_W ** -0.5)
    rel_bias = nrm((N_BUCKETS, SW_HEADS), 0.5)
    ffn_norm = gain((DEPTH, D))
    dense_w_gate = nrm((N_DENSE, D, D_FF), D ** -0.5)
    dense_w_up = nrm((N_DENSE, D, D_FF), D ** -0.5)
    dense_w_down = nrm((N_DENSE, D_FF, D), D_FF ** -0.5)
    moe_router = nrm((N_MOE, D, N_EXPERTS), D ** -0.5)
    moe_w_gate = nrm((N_MOE, N_EXPERTS, D, D_FF), D ** -0.5)
    moe_w_up = nrm((N_MOE, N_EXPERTS, D, D_FF), D ** -0.5)
    moe_w_down = nrm((N_MOE, N_EXPERTS, D_FF, D), D_FF ** -0.5)
    return {"x": x, "a_norm": a_norm, "a_w_in": a_w_in, "a_conv": a_conv,
            "a_log_decay": a_log_decay, "a_dt_bias": a_dt_bias, "a_out_norm": a_out_norm,
            "a_w_out": a_w_out, "kv_norm": kv_norm, "kv_w": kv_w, "k_norm": k_norm,
            "b_norm": b_norm, "b_w_q": b_w_q, "q_norm": q_norm, "b_sinks": b_sinks,
            "b_w_o": b_w_o, "rel_bias": rel_bias, "ffn_norm": ffn_norm,
            "dense_w_gate": dense_w_gate, "dense_w_up": dense_w_up, "dense_w_down": dense_w_down,
            "moe_router": moe_router, "moe_w_gate": moe_w_gate, "moe_w_up": moe_w_up,
            "moe_w_down": moe_w_down}

def reference(x, a_norm, a_w_in, a_conv, a_log_decay, a_dt_bias, a_out_norm, a_w_out,
              kv_norm, kv_w, k_norm, b_norm, b_w_q, q_norm, b_sinks, b_w_o, rel_bias,
              ffn_norm, dense_w_gate, dense_w_up, dense_w_down,
              moe_router, moe_w_gate, moe_w_up, moe_w_down):
    h = x
    k_sh = None
    v_sh = None
    for layer in range(DEPTH):
        if layer < N_A:
            i = layer
            h = h + gated_deltanet(rms_norm(h, a_norm[i]), a_w_in[i], a_conv[i], a_log_decay[i],
                                   a_dt_bias[i], a_out_norm[i], a_w_out[i])
        else:
            j = layer - N_A
            if j == 0:
                k_sh, v_sh = shared_kv(h, kv_norm, kv_w, k_norm)
            h = h + sliding_window_attention(rms_norm(h, b_norm[j]), k_sh, v_sh, b_w_q[j],
                                             q_norm[j], b_sinks[j], rel_bias, b_w_o[j])
        hn = rms_norm(h, ffn_norm[layer])
        if layer % 2 == 0:
            e = layer // 2
            h = h + swiglu(hn, dense_w_gate[e], dense_w_up[e], dense_w_down[e])
        else:
            e = layer // 2
            h = h + moe_swiglu(hn, moe_router[e], moe_w_gate[e], moe_w_up[e], moe_w_down[e])
    return h


_drawn_inputs = setup_inputs


def setup_inputs(seed=0):
    import zlib

    import numpy as np

    out = dict(_drawn_inputs(seed))
    spreads = {}
    factors = {'k_norm': 4.7, 'b_norm': 5.383, 'q_norm': 8.0, 'b_sinks': 22.081}
    for name, (base, spread) in spreads.items():
        noise = np.random.default_rng([zlib.crc32(name.encode()), seed]).standard_normal(out[name].shape)
        drawn = base * np.exp(spread * noise) if base else spread * noise
        out[name] = __import__('jax').numpy.asarray(drawn.astype(out[name].dtype))
    for name, factor in factors.items():
        out[name] = (out[name] * factor).astype(out[name].dtype)
    return out
```

```python
from contextlib import ExitStack

import concourse.bass as bass
from concourse import mybir
import numpy as np

F32 = mybir.dt.float32
I32 = mybir.dt.int32
U32 = mybir.dt.uint32
ALU = mybir.AluOpType
ACT = mybir.ActivationFunctionType
AX = mybir.AxisListType.X

P = 128
D = 1024
KT = D // P
S = 256
TT = S // P
HEADS = 8
QKV = 3 * D
CH = 64
NCH = S // CH
UN = TT * HEADS
SW_HEADS, SW_KV, HD = 16, 4, 64
FF = 3584
FS = 512
NSL = FF // FS
EXPERTS = 8
WIN = 96
NWIN = -(-S // WIN)
ITEMS = NWIN * EXPERTS
SLOTS = 7
EPS = 1e-6
NEG = -1e30
N_BUCKETS, MAX_DIST = 32, 128
FL = 384

U_IN, U_OUT, U_FF = 0, 8, 10
U_KV = U_FF + 3 * NSL
U_Q, U_O = U_KV + 1, U_KV + 3
U_MOE = U_KV + 5


def g_unit(j):
    return 0 if j == 0 else 3 * j - 1


def d_unit(j):
    return 3 * j + 4 if j < NSL - 1 else 3 * NSL - 1


def ffn_sequence():
    seq = {}
    for j in range(NSL):
        seq[g_unit(j)] = ("gate", j)
        seq[g_unit(j) + 1] = ("up", j)
        seq[d_unit(j)] = ("down", j)
    return [seq[i] for i in range(3 * NSL)]


def constants():
    i = np.arange(P)
    same = (i[:, None] // CH) == (i[None, :] // CH)
    c = {
        "ident": np.eye(P),
        "ones": np.ones((P, P)),
        "up_incl": (i[:, None] <= i[None, :]) & same,
        "same_chunk": same,
        "before": i[:, None] < i[None, :],
        "iota_win": np.tile(np.arange(WIN), (P, 1)),
        "iota_item": np.tile(np.arange(ITEMS) // EXPERTS * WIN, (P, 1)),
        "neg_half": np.full((P, 32), -0.5),
        "iota8": np.tile(np.arange(EXPERTS), (P, 1)),
    }
    main = np.concatenate([np.asarray(v, np.float32) for v in c.values()], axis=1)
    at, off = {}, 0
    for k, v in c.items():
        at[k] = (off, off + v.shape[1])
        off += v.shape[1]
    levels = []
    b = 1
    while b < CH:
        s, t = i[:, None], i[None, :]
        levels.append((s // (2 * b) == t // (2 * b)) & (s // b % 2 == 0) & (t // b % 2 == 1))
        b *= 2
    levels = np.concatenate(levels, axis=1).astype(np.float32)
    dist = 2 * P - 1 - np.arange(FL)
    n = np.maximum(dist, 0)
    exact = N_BUCKETS // 2
    large = exact + (np.log(np.maximum(n, 1).astype(np.float32) / exact) / np.log(MAX_DIST / exact)
                     * (N_BUCKETS - exact)).astype(np.int32)
    bucket = np.where(n < exact, n, np.minimum(large, N_BUCKETS - 1))
    ok = (dist >= 0) & (dist < P)
    table = np.zeros((N_BUCKETS + 1, FL), np.float32)
    for col in range(FL):
        if ok[col]:
            table[bucket[col], col] = 1.0
        else:
            table[N_BUCKETS, col] = NEG
    return main, at, levels, table


def build(nc, x, a_norm, a_w_in, a_conv, a_log_decay, a_dt_bias, a_out_norm, a_w_out, kv_norm, kv_w,
          k_norm, b_norm, b_w_q, q_norm, b_sinks, b_w_o, rel_bias, ffn_norm, dense_w_gate,
          dense_w_up, dense_w_down, moe_router, moe_w_gate, moe_w_up, moe_w_down, c_main, c_levels,
          c_table, out, at):
    NC_MAIN = c_main.shape[1]
    NLEV = c_levels.shape[1] // P
    with ExitStack() as ctx:
        def sb(name, shape, dt=F32):
            return ctx.enter_context(nc.sbuf_tensor(name, shape, dt))

        def sem(name):
            return ctx.enter_context(nc.semaphore(name))

        ring = sb("ring", [P, SLOTS, KT, FS])
        h = sb("h", [P, TT, D])
        BS = TT * D
        hs = sb("hs", [P, BS])
        hnT = sb("hnT", [P, BS])
        cbuf = sb("cbuf", [P, 3, BS])
        zbuf = sb("zbuf", [P, BS])
        xbuf = sb("xbuf", [P, 4, BS])
        cst = sb("cst", [P, NC_MAIN])
        gcol = sb("gcol", [P, 43])
        cw = sb("cw", [P, 96])
        small = sb("small", [P, 344])
        bcv = sb("bcv", [P, 32])
        idx = sb("idx", [P, TT, 8], U32)
        flag = sb("flag", [1, 8], I32)
        fstage = sb("fstage", [SW_HEADS, FL])

        bk = [ctx.enter_context(nc.psum_tensor(f"bank{i}", [P, 512], F32)) for i in range(8)]
        bias_dram = nc.dram_tensor("bias_table", (SW_HEADS, FL), F32, kind="Internal")

        def C(name, rows=P):
            a, b = at[name]
            return cst[0:rows, a:b]

        ident, ones = C("ident"), C("ones")

        def as_units(ap):
            return ap.rearrange("p (u d) -> p u d", d=P)

        def blocks(ap):
            if len(ap.shape) == 3:
                return ap.rearrange("p k (n t) -> p (k n) t", t=P)
            return ap.rearrange("p (n t) -> p n t", t=P)

        def as_kt(ap):
            return ap.rearrange("p (k t) -> p k t", t=S)

        HNT = as_kt(hnT[:, :])
        HS = hs[:, :].rearrange("p (t d) -> p t d", d=D)
        CONV = cbuf[:, :, :].rearrange("p b (m t) -> p (b m) t", t=S)
        ZT = as_kt(zbuf[:, :])
        R = [as_units(ring[:, 3 + i // 2, 4 * (i % 2):4 * (i % 2) + 4, :].rearrange("p k f -> p (k f)"))
             for i in range(8)]
        X = [as_units(xbuf[:, i, :]) for i in range(4)]
        CB = [as_units(cbuf[:, i, :]) for i in range(3)]
        HSU = as_units(hs[:, :])
        LEV = hnT[:, 0:NLEV * P].rearrange("p (l c) -> p l c", c=P)
        rows1 = hs[0:96, 0:P]
        rows2 = hs[0:43, P:2 * P]
        wba = xbuf[:, 3, 0:KT * 16].rearrange("p (k n) -> p k n", n=16)
        dtb, alog, sinkb = bcv[:, 0:8], bcv[:, 8:16], bcv[:, 16:32]

        def sm(a, n):
            return small[:, a:a + n]

        DHT = cbuf[:, 0, :].rearrange("p (b i t) -> p b i t", b=2, i=4)
        DSG = cbuf[:, 1, 0:4 * S].rearrange("p (b t) -> p b t", b=4)
        KVW = SW_KV * HD
        RBW = xbuf[0:N_BUCKETS + 1, 2, 0:SW_HEADS]
        RBT = xbuf[0:N_BUCKETS + 1, 2, SW_HEADS:SW_HEADS + FL]
        KVNT = as_kt(xbuf[:, 2, :])
        KVT = zbuf[:, 0:D].rearrange("p (t n) -> p t n", t=TT)
        KD = zbuf[:, D:2 * D].rearrange("p (t g d) -> p t g d", t=TT, g=SW_KV)
        KTD = hnT[:, 0:SW_KV * S].rearrange("p (g t) -> p g t", t=S)
        KSQ = cbuf[:, 2, 0:TT * KVW].rearrange("p (t n) -> p t n", t=TT)
        QSQ = cbuf[:, 0, :].rearrange("p (t n) -> p t n", t=TT)
        QTOK = xbuf[:, 3, :].rearrange("p (t n) -> p t n", t=TT)
        QT = as_kt(cbuf[:, 1, :])
        PR = [cbuf[:, b, :].rearrange("p (a k) -> p a k", a=8) for b in (2, 0)]
        PTR = hs[:, :].rearrange("p (b a q) -> p b a q", b=2, a=8)
        BIAS = xbuf[:, 0:2, :].rearrange("p b (a k) -> p (b a) k", k=S)
        OTOK = xbuf[:, 2, :].rearrange("p (t n) -> p t n", t=TT)
        OT = as_kt(xbuf[:, 3, :])
        PT_FILLS = [0, 2, 4, 8, 12]
        ROUTER = small[:, 280:344].rearrange("p (k n) -> p k n", n=EXPERTS)
        MASK = sm(160, 16).rearrange("p (t e) -> p t e", e=EXPERTS)
        POS, GATE = (zbuf[:, i * TT * (ITEMS + 1):(i + 1) * TT * (ITEMS + 1)].rearrange("p (t e) -> p t e", t=TT)
                     for i in range(2))
        XT = xbuf[:, 0, 0:KT * WIN].rearrange("p (k s) -> p k s", s=WIN)
        PICK, PICKW = (xbuf[:, 1, i * TT * WIN:(i + 1) * TT * WIN].rearrange("p (t s) -> p t s", t=TT)
                       for i in range(2))
        PICKT = xbuf[:, 1, 4 * WIN:4 * WIN + S]
        OE = xbuf[:, 2, 0:D]
        MHT = xbuf[:, 3, 0:8 * WIN].rearrange("p (b i s) -> p b i s", b=2, i=4)
        MSG = xbuf[:, 3, 8 * WIN:12 * WIN].rearrange("p (b i s) -> p b i s", b=2, i=2)

        GA_FF0, GA_FF1, GA_KV, GA_B = 8, 16, 24, 32
        G_ON, G_Q, G_K = 40, 41, 42
        NORMS = [[(HNT, 0)], [(HNT, GA_FF0)], [(KVNT, GA_KV), (HNT, GA_B)], [(HNT, GA_FF1)]]

        cst_in, par_in, x_in, ba_in, lev_in = (sem(n) for n in ("cst_in", "par_in", "x_in", "ba_in", "lev_in"))
        slot_full = [sem(f"slot_full{i}") for i in range(SLOTS)]
        pow_in, pow_out = sem("pow_in"), sem("pow_out")
        v_seq, a_seq = sem("v_seq"), sem("a_seq")
        par_t, gcol_ready = sem("par_t"), sem("gcol_ready")
        hs_ready, tp_ready, hn_ready = sem("hs_ready"), sem("tp_ready"), sem("hn_ready")
        ba_ready, gate_v, gate_a, cum_ready, gb_ready, egb_ready, dt_ready = (
            sem(n) for n in ("ba_ready", "gate_v", "gate_a", "cum_ready", "gb_ready", "egb_ready", "dt_ready"))
        proj_mm, conv_done, silu_done, z_done = (sem(n) for n in ("proj_mm", "conv_done", "silu_done", "z_done"))
        tok_tp, tok_a, tok_v, scaled = (sem(n) for n in ("tok_tp", "tok_a", "tok_v", "scaled"))
        back_tp, back_a, back_v = (sem(n) for n in ("back_tp", "back_a", "back_v"))
        at_mm, at_ready, attn_mm, attn_ready = (sem(n) for n in ("at_mm", "at_ready", "attn_mm", "attn_ready"))
        b_ready, u_ready, t_tp, t_ready, y_mm, y_ready, z_mm = (
            sem(n) for n in ("b_ready", "u_ready", "t_tp", "t_ready", "y_mm", "y_ready", "z_mm"))
        uw_mm, uw_ready = sem("uw_mm"), sem("uw_ready")
        ws_mm, vn_ready, ks_mm, st_ready, o_mm, o_raw, o_norm, o_tp, og_ready = (
            sem(n) for n in ("ws_mm", "vn_ready", "ks_mm", "st_ready", "o_mm", "o_raw", "o_norm", "o_tp", "og_ready"))
        wo_mm, gu_mm, sg_ready, ht_ready, d_mm = (sem(n) for n in ("wo_mm", "gu_mm", "sg_ready", "ht_ready", "d_mm"))
        rb_one = sem("rb_one")
        rb_in, tb_mm, tb_ready, tb_out, bias_in = (sem(n) for n in ("rb_in", "tb_mm", "tb_ready", "tb_out", "bias_in"))
        kv_mm, q_mm, kvq_raw, k_scaled, q_scaled, kt_tp, kt_ready, qt_tp, qt_ready = (
            sem(n) for n in ("kv_mm", "q_mm", "kvq_raw", "k_scaled", "q_scaled", "kt_tp", "kt_ready", "qt_tp", "qt_ready"))
        sc_mm, sc_ready, mx_ready, ex_ready, pt_tp, pt_ready, av_mm, av_ready = (
            sem(n) for n in ("sc_mm", "sc_ready", "mx_ready", "ex_ready", "pt_tp", "pt_ready", "av_mm", "av_ready"))
        ot_tp, ot_ready, ao_mm = sem("ot_tp"), sem("ot_ready"), sem("ao_mm")
        rt_in, rt_mm, rt_ev, rt_ea, mask_ready, pos_mm, route_ready, flag_ready = (
            sem(n) for n in ("rt_in", "rt_mm", "rt_ev", "rt_ea", "mask_ready", "pos_mm", "route_ready", "flag_ready"))
        m_pick, m_gx, m_x, m_pt, m_pte, m_gu, m_sg, m_ht, m_d, m_oe, m_y, m_h = (
            sem(n) for n in ("m_pick", "m_gx", "m_x", "m_pt", "m_pte", "m_gu", "m_sg", "m_ht", "m_d", "m_oe", "m_y", "m_h"))
        stored = sem("stored")

        def cols(w, n):
            return w.rearrange("(k p) f -> p k f", p=P)[:, :, n * FS:(n + 1) * FS]

        def rows(w, n):
            return w[n * FS:(n + 1) * FS, :].rearrange("(i p) f -> p i f", p=P)

        def static_units():
            u = [("c", cols(a_w_in[0], n)) for n in range(8)]
            u += [("c", cols(a_w_out[0], n)) for n in range(2)]
            w = {"gate": dense_w_gate[0], "up": dense_w_up[0], "down": dense_w_down[0]}
            u += [("r", rows(w[k], j)) if k == "down" else ("c", cols(w[k], j)) for k, j in ffn_sequence()]
            u += [("c", cols(kv_w, 0))]
            u += [("c", cols(b_w_q[0], n)) for n in range(2)]
            u += [("c", cols(b_w_o[0], n)) for n in range(2)]
            return u

        def released(n):
            if n < U_OUT:
                return proj_mm, 2 * (n + 1)
            if n < U_FF:
                return wo_mm, 2 * (n - U_OUT + 1)
            if n < U_KV:
                kind, j = ffn_sequence()[n - U_FF]
                return (d_mm, j + 1) if kind == "down" else (gu_mm, 4 * (j + 1))
            if n < U_Q:
                return kv_mm, TT
            if n < U_O:
                return q_mm, TT * (n - U_Q + 1)
            return ao_mm, TT * (n - U_O + 1)

        def slot_c(s):
            return ring[:, s, :, :]

        def slot_r(s):
            return ring[:, s, :, :].rearrange("p k f -> p (k f)").rearrange("p (i f) -> p i f", f=D)

        def landed(eng, n):
            eng.wait_ge(slot_full[n % SLOTS], 16 * (n // SLOTS + 1))

        moe_w = {"gate": moe_w_gate[0], "up": moe_w_up[0], "down": moe_w_down[0]}

        def moe_src(kind, j, e):
            w = moe_w[kind][bass.ds(e, 1)]
            if kind == "down":
                return w[:, j * FS:(j + 1) * FS, :].rearrange("a (i p) f -> p (a i) f", p=P)
            return w.rearrange("a (k p) f -> p (a k) f", p=P)[:, :, j * FS:(j + 1) * FS]

        def moe_landed(eng, item, u):
            n = U_MOE + u
            eng.wait_ge(slot_full[n % SLOTS], 16 * (n // SLOTS + 1) + 16 * (3 * NSL // SLOTS) * item)

        def moe_released(u):
            kind, j = ffn_sequence()[u]
            return (m_d, NSL, j + 1) if kind == "down" else (m_gu, 2 * NSL, 2 * (j + 1))

        def load(eng, kind, src, s):
            dst = slot_r(s) if kind == "r" else slot_c(s)
            eng.dma_start(dst, src).then_inc(slot_full[s], 16)

        NPAR = 12
        block = ctx.enter_context(nc.Block())

        @block.sync
        def _(sp):
            units = static_units()
            sp.dma_start(h[:, :, :], x[0].rearrange("(t p) d -> p t d", p=P)).then_inc(x_in, 16)
            sp.dma_start(cst[:, :], c_main).then_inc(cst_in, 16)
            for n, (kind, src) in enumerate(units):
                if n >= SLOTS:
                    sp.wait_ge(*released(n - SLOTS))
                if n == U_FF:
                    sp.wait_ge(og_ready, 4)
                load(sp, kind, src, n % SLOTS)
            def expert_item(item, e, first):
                for u, (kind, j) in enumerate(ffn_sequence()):
                    n = U_MOE + u
                    if u >= SLOTS:
                        s, per, c = moe_released(u - SLOTS)
                        sp.wait_ge(s, per * item + c)
                    elif first:
                        sp.wait_ge(*released(n - SLOTS))
                    else:
                        s, per, c = moe_released(u - SLOTS + 3 * NSL)
                        sp.wait_ge(s, per * item + (c - per))
                    load(sp, "r" if kind == "down" else "c", moe_src(kind, j, e), n % SLOTS)

            expert_item(0, 0, True)
            with sp.Fori(1, EXPERTS) as e:
                expert_item(e, e, False)
            sp.wait_ge(flag_ready, 1)
            more = sp.value_load(flag[0:1, 0:1], min_val=0, max_val=S)
            with sp.If(more > WIN):
                with sp.Fori(1, NWIN) as w:
                    with sp.Fori(0, EXPERTS) as e:
                        expert_item(w * EXPERTS + e, e, False)
                sp.wait_ge(m_h, TT * 2 * ITEMS)
            sp.wait_ge(m_h, TT * 2 * EXPERTS)
            sp.dma_start(out[0].rearrange("(t p) d -> p t d", p=P), h[:, :, :]).then_inc(stored, 16)
            sp.wait_ge(stored, 16)

        @block.gpsimd
        def _(pool):
            pool.dma_start(rows1, a_conv[0].rearrange("j (m p) -> (j m) p", p=P)).then_inc(par_in, 16)
            for r0, src in ((0, a_norm[0]), (GA_FF0, ffn_norm[0]), (GA_FF1, ffn_norm[1]), (GA_KV, kv_norm),
                            (GA_B, b_norm[0])):
                pool.dma_start(rows2[r0:r0 + KT, :], src.rearrange("(m p) -> m p", p=P)).then_inc(par_in, 16)
            pool.dma_start(rows2[G_ON:G_ON + 1, :], a_out_norm).then_inc(par_in, 16)
            for r0, src in ((G_Q, q_norm), (G_K, k_norm.rearrange("(a d) -> a d", a=1))):
                for half in range(2):
                    pool.dma_start(rows2[r0:r0 + 1, half * HD:(half + 1) * HD], src).then_inc(par_in, 16)
            pool.dma_start(bcv[:, 0:8], a_dt_bias[0].partition_broadcast(P)).then_inc(par_in, 16)
            pool.dma_start(bcv[:, 8:16], a_log_decay[0].partition_broadcast(P)).then_inc(ba_in, 16)
            pool.dma_start(bcv[:, 16:32], b_sinks[0].partition_broadcast(P)).then_inc(ba_in, 16)
            pool.dma_start(wba, a_w_in[0].rearrange("(k p) f -> p k f", p=P)[:, :, QKV + D:QKV + D + 16]
                           ).then_inc(ba_in, 16)
            powers = [0]

            def power(ap):
                powers[0] += 1
                pool.wait_ge(pow_in, powers[0])
                pool.tensor_tensor(ap, ap, C("neg_half")[:, 0:ap.shape[1]], ALU.pow).then_inc(pow_out, 1)

            pool.wait_ge(cst_in, 16)
            power(sm(192, TT))
            pool.wait_ge(proj_mm, 16)
            pool.dma_start(hnT[:, 0:NLEV * P], c_levels).then_inc(lev_in, 16)
            power(sm(200, UN))
            power(sm(264, UN))
            for t in range(TT):
                power(sm(200 + t * HEADS, HEADS))
            pool.wait_ge(og_ready, 4)
            pool.memset(xbuf[N_BUCKETS:N_BUCKETS + 1, 2, 0:SW_HEADS], 1.0).then_inc(rb_one, 1)
            pool.dma_start(xbuf[0:N_BUCKETS, 2, 0:SW_HEADS], rel_bias).then_inc(rb_in, 16)
            pool.dma_start(xbuf[0:N_BUCKETS + 1, 2, SW_HEADS:SW_HEADS + FL], c_table).then_inc(rb_in, 16)
            pool.dma_start(ROUTER, moe_router[0].rearrange("(k p) n -> p k n", p=P)).then_inc(rt_in, 16)
            pool.wait_ge(rb_one, 1)
            power(sm(192, TT))
            power(sm(192, TT))
            pool.wait_ge(tb_ready, 1)
            pool.dma_start(bias_dram.ap(), fstage[:, :]).then_inc(tb_out, 16)
            pool.wait_ge(tb_out, 16)
            for g4 in range(4):
                hb, par = g4 // 2, g4 % 2
                src = bass.AP(bias_dram, (8 * hb + par) * FL, [[1, P], [2 * FL, 4], [1, 2 * P]])
                pool.dma_start(BIAS[:, 4 * g4:4 * g4 + 4, :], src).then_inc(bias_in, 16)
            power(sm(0, TT * SW_KV))
            power(sm(8, TT * SW_HEADS))
            power(sm(192, TT))

        @block.tensor
        def _(pe):
            def transpose(o, i, k=P):
                return pe.transpose(o, i, C("ident", k)[:, 0:k])

            def norm(n):
                pe.wait_ge(hs_ready, TT * (n + 1))
                for b in range(4):
                    for c in (2 * b, 2 * b + 1):
                        for t in range(TT):
                            m = transpose(bk[4 + b][:, (c % 2) * S + t * P:(c % 2) * S + (t + 1) * P],
                                          HS[:, t, c * P:(c + 1) * P])
                    m.then_inc(tp_ready, 1)
                pe.wait_ge(hn_ready, 4 * (n + 1))

            pe.wait_ge(cst_in, 16)
            pe.wait_ge(par_in, 16 * NPAR)
            transpose(bk[0][:, 0:96], rows1, 96)
            transpose(bk[0][:, 128:171], rows2, 43).then_inc(par_t, 1)
            norm(0)

            pe.wait_ge(ba_in, 48)
            for t in range(TT):
                for k in range(KT):
                    m = pe.matmul(bk[5][:, 16 * t:16 * t + 16], HNT[:, k, t * P:(t + 1) * P], wba[:, k, :],
                                  start=k == 0, stop=k == KT - 1)
            m.then_inc(ba_ready, 1)

            def project(f):
                u = f // 2
                if f % 2 == 0:
                    landed(pe, U_IN + u)
                if 4 <= f:
                    pe.wait_ge(conv_done, f - 3)
                for q in range(2):
                    c0 = (2 * (f % 2) + q) * P
                    for k in range(KT):
                        m = pe.matmul(bk[f % 4][:, q * S:(q + 1) * S], slot_c(u % SLOTS)[:, k, c0:c0 + P],
                                      HNT[:, k, :], start=k == 0, stop=k == KT - 1)
                m.then_inc(proj_mm, 1)

            for f in range(3):
                project(f)
            pe.wait_ge(gate_v, 2)
            pe.matmul(bk[6][:, 0:UN], C("up_incl"), sm(96, UN), start=True, stop=True)
            pe.matmul(bk[6][:, UN:2 * UN], C("same_chunk"), sm(96, UN), start=True, stop=True).then_inc(cum_ready, 1)
            for f in range(3, 6):
                project(f)
            pe.wait_ge(gate_v, 4)
            for q in range(4):
                pe.matmul(bk[4 + q][:, :], ones, X[0][:, 4 * q:4 * q + 4, :], start=True, stop=True
                          ).then_inc(gb_ready, 1)
            for f in range(6, 16):
                project(f)

            pe.wait_ge(silu_done, 12)
            pe.wait_ge(dt_ready, 4)
            for f in range(12):
                m0, g = (8, 0, 16)[f // 4], f % 4
                if f >= 4:
                    pe.wait_ge(tok_a, f - 3)
                for i in range(4):
                    u = 4 * g + i
                    m = transpose(bk[4 + g][:, i * P:(i + 1) * P],
                                  CONV[:, m0 + u % HEADS, (u // HEADS) * P:(u // HEADS + 1) * P])
                m.then_inc(tok_tp, 1)
            pe.wait_ge(z_done, 4)
            for f in range(12):
                src, g = (R[3], R[4], R[0])[f // 4], f % 4
                if f >= 4:
                    pe.wait_ge(back_a, f - 3)
                pe.wait_ge(scaled, g + 1 if f < 8 else g + 5)
                for i in range(4):
                    m = transpose(bk[g][:, i * P:(i + 1) * P], src[:, 4 * g + i, :])
                m.then_inc(back_tp, 1)
            for g in range(4):
                pe.wait_ge(back_a, 5 + g)
                pe.wait_ge(tok_v, g + 1)
                for u in range(4 * g, 4 * g + 4):
                    m = pe.matmul(bk[4 + g][:, (u % 4) * P:(u % 4 + 1) * P], CB[1][:, u, :], CB[2][:, u, :],
                                  start=True, stop=True)
                m.then_inc(at_mm, 1)
            for g in range(4):
                pe.wait_ge(back_v, g + 1)
                for u in range(4 * g, 4 * g + 4):
                    m = pe.matmul(bk[g][:, (u % 4) * P:(u % 4 + 1) * P], CB[1][:, u, :], CB[0][:, u, :],
                                  start=True, stop=True)
                m.then_inc(attn_mm, 1)

            def turn(lv):
                for g in range(4):
                    pe.wait_ge(u_ready, 4 * lv + g + 1)
                    if lv == 0:
                        pe.wait_ge(attn_ready, g + 1)
                    for u in range(4 * g, 4 * g + 4):
                        m = transpose(bk[g][:, (u % 4) * P:(u % 4 + 1) * P], R[3][:, u, :])
                    m.then_inc(t_tp, 1)

            turn(0)
            for lv in range(1, NLEV):
                for g in range(4):
                    pe.wait_ge(t_ready, 4 * (lv - 1) + g + 1)
                    pe.wait_ge(b_ready, 4 * (lv - 1) + g + 1)
                    for u in range(4 * g, 4 * g + 4):
                        m = pe.matmul(bk[g][:, (u % 4) * P:(u % 4 + 1) * P], X[0][:, u, :], R[4][:, u, :],
                                      start=True, stop=True)
                    m.then_inc(y_mm, 1)
                for g in range(4):
                    pe.wait_ge(y_ready, 4 * (lv - 1) + g + 1)
                    for u in range(4 * g, 4 * g + 4):
                        m = pe.matmul(bk[4 + g][:, (u % 4) * P:(u % 4 + 1) * P], X[3][:, u, :], R[3][:, u, :],
                                      start=True, stop=True)
                    m.then_inc(z_mm, 1)
                if lv < NLEV - 1:
                    turn(lv)
            for g in range(4):
                pe.wait_ge(u_ready, 4 * (NLEV - 1) + g + 1)
                for u in range(4 * g, 4 * g + 4):
                    m = pe.matmul(bk[4 + g][:, (u % 4) * P:(u % 4 + 1) * P], R[3][:, u, :], R[2][:, u, :],
                                  start=True, stop=True)
                m.then_inc(uw_mm, 1)
                for u in range(4 * g, 4 * g + 4):
                    m = pe.matmul(bk[g][:, (u % 4) * P:(u % 4 + 1) * P], R[5][:, u, :], R[3][:, u, :],
                                  start=True, stop=True)
                m.then_inc(uw_mm, 1)
            pe.wait_ge(uw_ready, 8)
            state = cbuf[:, 2, 0:HEADS * P].rearrange("p (h d) -> p h d", d=P)
            for i in range(NCH):
                t, r0 = i // 2, (i % 2) * CH
                rw = slice(r0, r0 + CH)
                if i > 0:
                    for b in range(2):
                        pe.wait_ge(st_ready, 2 * (i - 1) + b + 1)
                        for hh in range(4 * b, 4 * b + 4):
                            m = pe.matmul(bk[b][rw, (hh % 4) * P:(hh % 4 + 1) * P], CB[0][:, t * HEADS + hh, rw],
                                          state[:, hh, :], start=True, stop=True)
                        m.then_inc(ws_mm, 1)
                for b in range(2):
                    if i > 0:
                        pe.wait_ge(vn_ready, 2 * (i - 1) + b + 1)
                    if i == 2:
                        pe.wait_ge(o_raw, b + 1)
                    if i < NCH - 1:
                        for hh in range(4 * b, 4 * b + 4):
                            u = t * HEADS + hh
                            m = pe.matmul(bk[4 + 2 * (i % 2) + b][:, (hh % 4) * P:(hh % 4 + 1) * P],
                                          R[6][rw, u, :], HSU[rw, u, :], start=True, stop=True)
                        m.then_inc(ks_mm, 1)
                    for hh in range(4 * b, 4 * b + 4):
                        u = t * HEADS + hh
                        o = bk[2 + b][rw, (hh % 4) * P:(hh % 4 + 1) * P]
                        if i > 0:
                            pe.matmul(o, R[7][:, u, rw], state[:, hh, :], start=True, stop=False)
                        m = pe.matmul(o, R[0][rw, u, rw], HSU[rw, u, :], start=i == 0, stop=True)
                    m.then_inc(o_mm, 1)
            for t in range(TT):
                for b in range(2):
                    pe.wait_ge(o_norm, 2 * t + b + 1)
                    for hh in range(4 * b, 4 * b + 4):
                        m = transpose(bk[4 + 2 * t + b][:, (hh % 4) * P:(hh % 4 + 1) * P], X[0][:, t * HEADS + hh, :])
                    m.then_inc(o_tp, 1)
            pe.wait_ge(og_ready, 4)
            for n in range(2):
                landed(pe, U_OUT + n)
                for t in range(TT):
                    for k in range(KT):
                        m = pe.matmul(bk[2 * t + n][:, :], HNT[:, k, t * P:(t + 1) * P],
                                      slot_c((U_OUT + n) % SLOTS)[:, k, :], start=k == 0, stop=k == KT - 1)
                    m.then_inc(wo_mm, 1)
            norm(1)

            def gate_up(j):
                landed(pe, U_FF + g_unit(j))
                landed(pe, U_FF + g_unit(j) + 1)
                for i in range(4):
                    if j > 0:
                        pe.wait_ge(ht_ready, 4 * (j - 1) + i + 1)
                    for q in range(2):
                        w = slot_c((U_FF + g_unit(j) + q) % SLOTS)
                        for k in range(KT):
                            m = pe.matmul(bk[4 + i][:, q * S:(q + 1) * S], w[:, k, i * P:(i + 1) * P], HNT[:, k, :],
                                          start=k == 0, stop=k == KT - 1)
                    m.then_inc(gu_mm, 1)

            def down(j):
                landed(pe, U_FF + d_unit(j))
                w = slot_r((U_FF + d_unit(j)) % SLOTS)
                pe.wait_ge(ht_ready, 4 * (j + 1))
                for t in range(TT):
                    for n in range(2):
                        for i in range(4):
                            m = pe.matmul(bk[2 * t + n][:, :], DHT[:, j % 2, i, t * P:(t + 1) * P],
                                          w[:, i, n * FS:(n + 1) * FS], start=j == 0 and i == 0,
                                          stop=j == NSL - 1 and i == 3)
                m.then_inc(d_mm, 1)

            gate_up(0)
            for j in range(1, NSL):
                gate_up(j)
                down(j - 1)
            down(NSL - 1)
            pe.wait_ge(rb_in, 32)
            pe.wait_ge(rb_one, 1)
            pe.matmul(bk[4][0:SW_HEADS, 0:FL], RBW, RBT, start=True, stop=True).then_inc(tb_mm, 1)
            pe.wait_ge(tb_ready, 1)
            norm(2)

            landed(pe, U_KV)
            for t in range(TT):
                for k in range(KT):
                    m = pe.matmul(bk[t][:, :], KVNT[:, k, t * P:(t + 1) * P], slot_c(U_KV % SLOTS)[:, k, :],
                                  start=k == 0, stop=k == KT - 1)
                m.then_inc(kv_mm, 1)
            for n in range(2):
                landed(pe, U_Q + n)
                for t in range(TT):
                    for k in range(KT):
                        m = pe.matmul(bk[2 + 2 * n + t][:, :], HNT[:, k, t * P:(t + 1) * P],
                                      slot_c((U_Q + n) % SLOTS)[:, k, :], start=k == 0, stop=k == KT - 1)
                    m.then_inc(q_mm, 1)
            pe.wait_ge(k_scaled, 1)
            for g in range(SW_KV):
                for t in range(TT):
                    m = transpose(bk[6 + g // 2][:, (g % 2) * S + t * P:(g % 2) * S + (t + 1) * P], KD[:, t, g, :])
                if g % 2:
                    m.then_inc(kt_tp, 1)
            pe.wait_ge(q_scaled, 1)
            for b in range(4):
                for c in (2 * b, 2 * b + 1):
                    for t in range(TT):
                        m = transpose(bk[b][:, (c % 2) * S + t * P:(c % 2) * S + (t + 1) * P],
                                      QTOK[:, t, c * P:(c + 1) * P])
                m.then_inc(qt_tp, 1)
            pe.wait_ge(kt_ready, 2)
            pe.wait_ge(qt_ready, 4)

            def scores(b):
                n, hb = b // 2, b % 2
                k0, kw = (0, P) if n == 0 else (0, 2 * P)
                if b >= 1:
                    pe.wait_ge(sc_ready, b)
                for cc in range(4):
                    for par in range(2):
                        c = 4 * hb + cc
                        rw = slice(par * HD, (par + 1) * HD)
                        m = pe.matmul(bk[2 * par + cc // 2][:, (cc % 2) * S:(cc % 2) * S + kw],
                                      QT[rw, c, n * P:(n + 1) * P], KTD[rw, c // 2, k0:k0 + kw],
                                      start=True, stop=True)
                m.then_inc(sc_mm, 1)

            def weigh(b):
                n, hb = b // 2, b % 2
                nk = n + 1
                pe.wait_ge(ex_ready, b + 1)
                for kb in range(nk):
                    for q in range(2):
                        fills = PT_FILLS[b] + 2 * kb + q
                        if fills >= 2:
                            pe.wait_ge(pt_ready, fills - 1)
                        for a in range(4 * q, 4 * q + 4):
                            m = transpose(bk[4 + q][:, (a % 4) * P:(a % 4 + 1) * P],
                                          PR[b % 2][:, a, kb * P:(kb + 1) * P])
                        m.then_inc(pt_tp, 1)
                pe.wait_ge(pt_ready, PT_FILLS[b + 1])
                if b >= 1:
                    pe.wait_ge(av_ready, b)
                for a in range(8):
                    par, cc = a // 4, a % 4
                    g = (4 * hb + cc) // 2
                    for kb in range(nk):
                        m = pe.matmul(bk[6][:, a * HD:(a + 1) * HD], PTR[:, kb, a, :],
                                      KVT[:, kb, KVW + g * HD:KVW + (g + 1) * HD], start=kb == 0, stop=kb == nk - 1)
                m.then_inc(av_mm, 1)

            scores(0)
            for b in range(1, 4):
                scores(b)
                weigh(b - 1)
            weigh(3)
            pe.wait_ge(av_ready, 4)
            for b in range(4):
                for c in (2 * b, 2 * b + 1):
                    for t in range(TT):
                        m = transpose(bk[b][:, (c % 2) * S + t * P:(c % 2) * S + (t + 1) * P],
                                      OTOK[:, t, c * P:(c + 1) * P])
                m.then_inc(ot_tp, 1)
            pe.wait_ge(ot_ready, 4)
            for n in range(2):
                landed(pe, U_O + n)
                for t in range(TT):
                    for k in range(KT):
                        m = pe.matmul(bk[4 + 2 * t + n][:, :], OT[:, k, t * P:(t + 1) * P],
                                      slot_c((U_O + n) % SLOTS)[:, k, :], start=k == 0, stop=k == KT - 1)
                    m.then_inc(ao_mm, 1)
            norm(3)

            pe.wait_ge(rt_in, 16)
            for t in range(TT):
                for k in range(KT):
                    m = pe.matmul(bk[0][:, 8 * t:8 * t + 8], HNT[:, k, t * P:(t + 1) * P], ROUTER[:, k, :],
                                  start=k == 0, stop=k == KT - 1)
            m.then_inc(rt_mm, 1)
            pe.wait_ge(mask_ready, 1)
            pe.matmul(bk[1][:, 0:8], C("before"), MASK[:, 0, :], start=True, stop=True)
            pe.matmul(bk[1][:, 8:16], ones, MASK[:, 0, :], start=True, stop=False)
            pe.matmul(bk[1][:, 8:16], C("before"), MASK[:, 1, :], start=False, stop=True)
            pe.matmul(bk[1][:, 16:24], ones, MASK[:, 0, :], start=True, stop=False)
            pe.matmul(bk[1][:, 16:24], ones, MASK[:, 1, :], start=False, stop=True).then_inc(pos_mm, 1)

            def gather(item, first):
                pe.wait_ge(m_pick, item + 1)
                for q in range(2):
                    for c in range(4 * q, 4 * q + 4):
                        for t in range(TT):
                            m = pe.matmul(bk[6 + q][:, (c % 4) * WIN:(c % 4 + 1) * WIN], HS[:, t, c * P:(c + 1) * P],
                                          PICK[:, t, :], start=t == 0, stop=t == TT - 1)
                    m.then_inc(m_gx, 1)
                if not first:
                    pe.wait_ge(m_pte, item)
                for t in range(TT):
                    m = transpose(bk[5][0:WIN, t * P:(t + 1) * P], PICKW[:, t, :])
                m.then_inc(m_pt, 1)

            def m_gate_up(item, j, first):
                moe_landed(pe, item, g_unit(j))
                moe_landed(pe, item, g_unit(j) + 1)
                for b in range(2):
                    f = 2 * j + b
                    if not (first and f < 2):
                        pe.wait_ge(m_ht, 2 * NSL * item + (f - 1))
                    for i in (2 * b, 2 * b + 1):
                        for q in range(2):
                            w = slot_c((U_MOE + g_unit(j) + q) % SLOTS)
                            c0 = ((i % 2) * 2 + q) * WIN
                            for k in range(KT):
                                m = pe.matmul(bk[2 + f % 2][:, c0:c0 + WIN], w[:, k, i * P:(i + 1) * P],
                                              XT[:, k, :], start=k == 0, stop=k == KT - 1)
                    m.then_inc(m_gu, 1)

            def m_down(item, j, first):
                moe_landed(pe, item, d_unit(j))
                pe.wait_ge(m_ht, 2 * NSL * item + 2 * (j + 1))
                if j == 0 and not first:
                    pe.wait_ge(m_h, 4 * item)
                w = slot_r((U_MOE + d_unit(j)) % SLOTS)
                for n in range(2):
                    for i in range(4):
                        m = pe.matmul(bk[n][0:WIN, :], MHT[:, j % 2, i, :], w[:, i, n * FS:(n + 1) * FS],
                                      start=j == 0 and i == 0, stop=j == NSL - 1 and i == 3)
                m.then_inc(m_d, 1)

            def expert(item, first=False):
                pe.wait_ge(m_x, 2 * item + 2)
                m_gate_up(item, 0, first)
                for j in range(1, NSL):
                    m_gate_up(item, j, first)
                    m_down(item, j - 1, first)
                gather(item + 1, False)
                m_down(item, NSL - 1, first)
                pe.wait_ge(m_oe, 2 * item + 2)
                pe.wait_ge(m_pte, item + 1)
                for t in range(TT):
                    for n in range(2):
                        if t > 0:
                            pe.wait_ge(m_h, 4 * item + n + 1)
                        pe.matmul(bk[(4, 1)[n]][:, :], PICKT[0:WIN, t * P:(t + 1) * P],
                                  OE[0:WIN, n * FS:(n + 1) * FS], start=True, stop=True).then_inc(m_y, 1)

            gather(0, True)
            expert(0, first=True)
            with pe.Fori(1, EXPERTS) as e:
                expert(e)
            pe.wait_ge(flag_ready, 1)
            more = pe.value_load(flag[0:1, 0:1], min_val=0, max_val=S)
            with pe.If(more > WIN):
                with pe.Fori(EXPERTS, ITEMS) as e:
                    expert(e)

        @block.scalar
        def _(act):
            count = [0]

            def then(ins):
                count[0] += 1
                ins.then_inc(a_seq, 1)
                act.wait_ge(a_seq, count[0])

            def norm(n):
                for b in (1, 3):
                    act.wait_ge(tp_ready, 4 * n + b + 1)
                    for dst, g0 in NORMS[n]:
                        for c in (2 * b, 2 * b + 1):
                            last = act.activation(dst[:, c, :], bk[4 + b][:, (c % 2) * S:(c % 2 + 1) * S], ACT.Copy,
                                                  scale=gcol[:, g0 + c:g0 + c + 1])
                    last.then_inc(hn_ready, 1)

            act.wait_ge(gcol_ready, 1)
            norm(0)
            act.wait_ge(gate_v, 1)
            act.activation(sm(32, UN), sm(0, UN), ACT.Exp)
            act.activation(sm(128, 8), alog, ACT.Exp)
            then(act.activation(sm(48, UN), sm(16, UN), ACT.Exp))
            act.activation(sm(64, UN), sm(48, UN), ACT.Ln, bias=1.0).then_inc(gate_a, 1)
            act.wait_ge(gate_v, 3)
            act.activation(sm(144, UN), sm(112, UN), ACT.Exp)
            act.activation(sm(176, UN), sm(160, UN), ACT.Exp).then_inc(gate_a, 1)
            for q in range(4):
                act.wait_ge(gb_ready, q + 1)
                act.activation(X[1][:, 4 * q:4 * q + 4, :], bk[4 + q][:, :].rearrange("p (u c) -> p u c", c=P),
                               ACT.Exp).then_inc(egb_ready, 1)
            for q in range(4):
                act.wait_ge(dt_ready, q + 1)
                act.activation(X[2][:, 4 * q:4 * q + 4, :], X[2][:, 4 * q:4 * q + 4, :], ACT.Exp
                               ).then_inc(gate_a, 1)
            for f in range(12):
                act.wait_ge(conv_done, f + 1)
                act.activation(CONV[:, 2 * f:2 * f + 2, :], CONV[:, 2 * f:2 * f + 2, :], ACT.Silu
                               ).then_inc(silu_done, 1)
            for f in range(12, 16):
                act.wait_ge(proj_mm, f + 1)
                act.activation(ZT[:, 2 * (f - 12):2 * (f - 12) + 2, :],
                               bk[f % 4][:, :].rearrange("p (m t) -> p m t", t=S), ACT.Silu).then_inc(z_done, 1)
            for f in range(8):
                raw, sq = ((R[1], X[0]), (R[0], X[3]))[f // 4]
                g = f % 4
                act.wait_ge(tok_tp, f + 1)
                src = bk[4 + g][:, :].rearrange("p (u c) -> p u c", c=P)
                act.activation(raw[:, 4 * g:4 * g + 4, :], src, ACT.Copy)
                act.activation(sq[:, 4 * g:4 * g + 4, :], src, ACT.Square).then_inc(tok_a, 1)
            for f in range(8):
                g = f % 4
                act.wait_ge(back_tp, f + 1)
                act.activation(CB[1 + f // 4][:, 4 * g:4 * g + 4, :],
                               bk[g][:, :].rearrange("p (u c) -> p u c", c=P), ACT.Copy).then_inc(back_a, 1)
            for g in range(4):
                act.wait_ge(t_tp, g + 1)
                act.activation(R[4][:, 4 * g:4 * g + 4, :], bk[g][:, :].rearrange("p (u c) -> p u c", c=P),
                               ACT.Copy).then_inc(t_ready, 1)
            for lv in range(1, NLEV):
                for g in range(4):
                    act.wait_ge(y_mm, 4 * (lv - 1) + g + 1)
                    act.activation(X[3][:, 4 * g:4 * g + 4, :], bk[g][:, :].rearrange("p (u c) -> p u c", c=P),
                                   ACT.Copy).then_inc(y_ready, 1)
                if lv < NLEV - 1:
                    for g in range(4):
                        act.wait_ge(t_tp, 4 * lv + g + 1)
                        act.activation(R[4][:, 4 * g:4 * g + 4, :], bk[g][:, :].rearrange("p (u c) -> p u c", c=P),
                                       ACT.Copy).then_inc(t_ready, 1)
            for f in range(8):
                g = f // 2
                act.wait_ge(uw_mm, f + 1)
                dst, b = (HSU, 4 + g) if f % 2 == 0 else (CB[0], g)
                act.activation(dst[:, 4 * g:4 * g + 4, :], bk[b][:, :].rearrange("p (u c) -> p u c", c=P),
                               ACT.Copy).then_inc(uw_ready, 1)
            for t in range(TT):
                for b in range(2):
                    act.wait_ge(o_mm, 4 * t + 2 + b + 1)
                    src = bk[2 + b][:, :].rearrange("p (u c) -> p u c", c=P)
                    u0 = t * HEADS + 4 * b
                    act.activation(X[0][:, u0:u0 + 4, :], src, ACT.Copy)
                    act.activation(X[3][:, u0:u0 + 4, :], src, ACT.Square).then_inc(o_raw, 1)
            norm(1)
            for f in range(4 * NSL):
                act.wait_ge(gu_mm, f + 1)
                if f >= 4:
                    act.wait_ge(ht_ready, f - 3)
                act.activation(DSG[:, f % 4, :], bk[4 + f % 4][:, 0:S], ACT.Silu).then_inc(sg_ready, 1)
            norm(2)
            for t in range(TT):
                act.wait_ge(kv_mm, t + 1)
                act.activation(KVT[:, t, :], bk[t][:, :], ACT.Copy)
                act.activation(KSQ[:, t, :], bk[t][:, 0:KVW], ACT.Square).then_inc(kvq_raw, 1)
            for n in range(2):
                for t in range(TT):
                    act.wait_ge(q_mm, 2 * n + t + 1)
                    b = bk[2 + 2 * n + t]
                    act.activation(QTOK[:, t, n * FS:(n + 1) * FS], b[:, :], ACT.Copy)
                    act.activation(QSQ[:, t, n * FS:(n + 1) * FS], b[:, :], ACT.Square).then_inc(kvq_raw, 1)
            for b in range(2):
                act.wait_ge(kt_tp, b + 1)
                act.activation(KTD[:, 2 * b:2 * b + 2, :], bk[6 + b][:, :].rearrange("p (g t) -> p g t", t=S), ACT.Copy,
                               scale=gcol[:, G_K:G_K + 1]).then_inc(kt_ready, 1)
            for b in range(4):
                n = b // 2
                kw = (n + 1) * P
                act.wait_ge(mx_ready, b + 1)
                for a in range(8):
                    act.activation(PR[b % 2][:, a, 0:kw], PR[b % 2][:, a, 0:kw], ACT.Exp,
                                   bias=sm(80 + a, 1), accum_out=sm(96 + 8 * (b % 2) + a, 1))
                act.activation(sm(112 + 8 * (b % 2), 8), sm(88, 8), ACT.Exp).then_inc(ex_ready, 1)
                for f in range(PT_FILLS[b], PT_FILLS[b + 1]):
                    kb, q = (f - PT_FILLS[b]) // 2, f % 2
                    act.wait_ge(pt_tp, f + 1)
                    if f == PT_FILLS[b] and b >= 1:
                        act.wait_ge(av_mm, b)
                    act.activation(PTR[:, kb, 4 * q:4 * q + 4, :], bk[4 + q][:, :].rearrange("p (u c) -> p u c", c=P),
                                   ACT.Copy).then_inc(pt_ready, 1)
            for b in (1, 3):
                act.wait_ge(ot_tp, b + 1)
                act.activation(blocks(OT[:, 2 * b:2 * b + 2, :])[:, :, ::-1], blocks(bk[b][:, :]),
                               ACT.Copy).then_inc(ot_ready, 1)
            norm(3)
            act.wait_ge(rt_ev, 1)
            act.activation(sm(2, 2), sm(0, 2), ACT.Exp).then_inc(rt_ea, 1)

            def expert(item, first=False):
                act.wait_ge(m_pt, item + 1)
                if not first:
                    act.wait_ge(m_y, 4 * item)
                act.activation(PICKT[0:WIN, :], bk[5][0:WIN, 0:S], ACT.Copy).then_inc(m_pte, 1)
                for f in range(2 * NSL):
                    act.wait_ge(m_gu, 2 * NSL * item + f + 1)
                    if not (first and f < 2):
                        act.wait_ge(m_ht, 2 * NSL * item + f - 1)
                    b = bk[2 + f % 2][:, 0:4 * WIN].rearrange("p (i q s) -> p i q s", i=2, q=2)
                    act.activation(MSG[:, f % 2, :, :], b[:, :, 0, :], ACT.Silu).then_inc(m_sg, 1)
                for n in range(2):
                    act.wait_ge(m_d, NSL * item + NSL)
                    act.activation(OE[0:WIN, n * FS:(n + 1) * FS], bk[n][0:WIN, :], ACT.Copy).then_inc(m_oe, 1)

            expert(0, first=True)
            with act.Fori(1, EXPERTS) as e:
                expert(e)
            act.wait_ge(flag_ready, 1)
            more = act.value_load(flag[0:1, 0:1], min_val=0, max_val=S)
            with act.If(more > WIN):
                with act.Fori(EXPERTS, ITEMS) as e:
                    expert(e)

        @block.vector
        def _(dve):
            count = [0]
            powers = [0]

            def then(ins):
                count[0] += 1
                ins.then_inc(v_seq, 1)
                dve.wait_ge(v_seq, count[0])

            def bc(ap, n):
                return ap.unsqueeze(2).to_broadcast([P, ap.shape[1], n])

            def over(ap, m):
                return ap.unsqueeze(1).to_broadcast([P, m, ap.shape[1]])

            def power(ap, eps):
                powers[0] += 1
                dve.tensor_scalar(ap, ap, float(eps), None, ALU.add).then_inc(pow_in, 1)
                dve.wait_ge(pow_out, powers[0])

            def norm_in(n):
                for t in range(TT):
                    last = dve.tensor_tensor_reduce(out=HS[:, t, :], in0=h[:, t, :], in1=h[:, t, :], scale=1.0,
                                                    scalar=0.0, op0=ALU.mult, op1=ALU.add,
                                                    accum_out=sm(192 + t, 1))
                then(last)
                power(sm(192, TT), D * EPS)
                for t in range(TT):
                    dve.tensor_scalar(HS[:, t, :], h[:, t, :], sm(192 + t, 1), float(D) ** 0.5, ALU.mult, ALU.mult
                                      ).then_inc(hs_ready, 1)

            def norm_out(n):
                for b in (0, 2):
                    dve.wait_ge(tp_ready, 4 * n + b + 1)
                    for dst, g0 in NORMS[n]:
                        for c in (2 * b, 2 * b + 1):
                            last = dve.tensor_scalar(dst[:, c, :], bk[4 + b][:, (c % 2) * S:(c % 2 + 1) * S],
                                                     gcol[:, g0 + c:g0 + c + 1], None, ALU.mult)
                    last.then_inc(hn_ready, 1)

            def add_to_h(b, t, n):
                hh = h[:, t, n * FS:(n + 1) * FS]
                return dve.tensor_tensor(hh, hh, bk[b][:, :], ALU.add)

            dve.wait_ge(par_t, 1)
            dve.tensor_copy(cw[:, :], bk[0][:, 0:96])
            dve.tensor_copy(gcol[:, :], bk[0][:, 128:171]).then_inc(gcol_ready, 1)
            dve.wait_ge(gcol_ready, 1)
            dve.wait_ge(x_in, 16)
            norm_in(0)
            norm_out(0)
            dve.wait_ge(ba_ready, 1)
            ba = bk[5][:, 0:2 * UN].rearrange("p (t n) -> p t n", n=2 * HEADS)

            def u2(a):
                return sm(a, UN).rearrange("p (t h) -> p t h", h=HEADS)

            dve.tensor_scalar(u2(0), ba[:, :, 0:HEADS], -1.0, None, ALU.mult)
            then(dve.tensor_tensor(u2(80), ba[:, :, HEADS:2 * HEADS], over(dtb, TT), ALU.add))
            then(dve.tensor_scalar(sm(16, UN), sm(80, UN), -1.0, None, ALU.mult))
            dve.tensor_tensor(sm(16, UN), sm(16, UN), sm(80, UN), ALU.min).then_inc(gate_v, 1)
            dve.wait_ge(gate_a, 1)
            dve.tensor_scalar(sm(0, UN), sm(32, UN), 1.0, None, ALU.add)
            then(dve.tensor_scalar(sm(80, UN), sm(80, UN), 0.0, None, ALU.max))
            dve.reciprocal(sm(32, UN), sm(0, UN))
            then(dve.tensor_tensor(sm(80, UN), sm(80, UN), sm(64, UN), ALU.add))
            dve.scalar_tensor_tensor(out=u2(96), in0=u2(80), scalar=-1.0, in1=over(sm(128, 8), TT), op0=ALU.mult,
                                     op1=ALU.mult).then_inc(gate_v, 1)

            def conv(f):
                dve.wait_ge(proj_mm, f + 1)
                b = bk[f % 4]
                for q in range(2):
                    m = 2 * f + q
                    last = dve.tensor_scalar(CONV[:, m, :], b[:, q * S:(q + 1) * S], cw[:, 72 + m:73 + m], None,
                                             ALU.mult)
                for lag in range(1, 4):
                    then(last)
                    for q in range(2):
                        m = 2 * f + q
                        tap = (3 - lag) * 24 + m
                        last = dve.scalar_tensor_tensor(
                            out=CONV[:, m, lag:S], in0=b[:, q * S:(q + 1) * S - lag], scalar=cw[:, tap:tap + 1],
                            in1=CONV[:, m, lag:S], op0=ALU.mult, op1=ALU.add)
                last.then_inc(conv_done, 1)

            conv(0)
            conv(1)
            dve.wait_ge(cum_ready, 1)
            then(dve.tensor_copy(sm(112, UN), bk[6][:, 0:UN]))
            dve.tensor_tensor(sm(160, UN), bk[6][:, UN:2 * UN], sm(112, UN), ALU.subtract).then_inc(gate_v, 1)
            for u in range(UN):
                last = dve.tensor_scalar(X[0][:, u, :], ident, sm(112 + u, 1), None, ALU.mult)
            last.then_inc(gate_v, 1)
            conv(2)
            conv(3)
            for q in range(4):
                dve.wait_ge(egb_ready, q + 1)
                for i in range(4):
                    u = 4 * q + i
                    last = dve.tensor_scalar(X[2][:, u, :], bk[4 + q][:, i * P:(i + 1) * P], sm(112 + u, 1), 0.0,
                                             ALU.subtract, ALU.min)
                last.then_inc(dt_ready, 1)
            for f in range(4, 12):
                conv(f)
            for q in range(4):
                dve.wait_ge(gate_a, 3 + q)
                last = dve.tensor_tensor(X[2][:, 4 * q:4 * q + 4, :], X[2][:, 4 * q:4 * q + 4, :],
                                         over(C("up_incl"), 4), ALU.mult)
            then(last)
            beta, eg, etail = sm(32, UN), sm(144, UN), sm(176, UN)
            rk, rkb, rkbe, rkt, rq = (sm(200 + 16 * i, UN) for i in range(4 + 1))
            for g in range(4):
                dve.wait_ge(tok_a, g + 1)
                last = dve.tensor_reduce(rk[:, 4 * g:4 * g + 4], X[0][:, 4 * g:4 * g + 4, :], AX, ALU.add)
            then(last)
            power(rk, EPS)
            dve.tensor_tensor(rkb, rk, beta, ALU.mult)
            then(dve.tensor_tensor(rkt, rk, etail, ALU.mult))
            then(dve.tensor_tensor(rkbe, rkb, eg, ALU.mult))
            for g in range(4):
                for u in range(4 * g, 4 * g + 4):
                    for dst, r in ((3, rk), (4, rkb), (5, rkbe), (6, rkt)):
                        last = dve.tensor_scalar(R[dst][:, u, :], R[1][:, u, :], r[:, u:u + 1], None, ALU.mult)
                last.then_inc(scaled, 1)
            for g in range(4):
                dve.wait_ge(tok_a, g + 5)
                last = dve.tensor_reduce(rq[:, 4 * g:4 * g + 4], X[3][:, 4 * g:4 * g + 4, :], AX, ALU.add)
            then(last)
            power(rq, EPS)
            for g in range(4):
                for u in range(4 * g, 4 * g + 4):
                    last = dve.tensor_scalar(R[0][:, u, :], R[0][:, u, :], rq[:, u:u + 1], float(P) ** -0.5,
                                             ALU.mult, ALU.mult)
                last.then_inc(scaled, 1)
            for g in range(4):
                dve.wait_ge(tok_tp, 9 + g)
                last = dve.tensor_tensor(R[2][:, 4 * g:4 * g + 4, :], bk[4 + g][:, :].rearrange("p (u c) -> p u c", c=P),
                                         bc(beta[:, 4 * g:4 * g + 4], P), ALU.mult)
                last.then_inc(tok_v, 1)
            for g in range(4):
                dve.wait_ge(back_tp, 9 + g)
                src = bk[g][:, :].rearrange("p (u c) -> p u c", c=P)
                dve.tensor_copy(CB[0][:, 4 * g:4 * g + 4, :], src)
                dve.tensor_tensor(R[7][:, 4 * g:4 * g + 4, :], src, X[1][:, 4 * g:4 * g + 4, :], ALU.mult
                                  ).then_inc(back_v, 1)
            dve.wait_ge(lev_in, 16)
            for g in range(4):
                dve.wait_ge(at_mm, g + 1)
                gs = slice(4 * g, 4 * g + 4)
                then(dve.tensor_tensor(R[1][:, gs, :], bk[4 + g][:, :].rearrange("p (u c) -> p u c", c=P),
                                       X[2][:, gs, :], ALU.mult))
                then(dve.tensor_tensor(X[0][:, gs, :], R[1][:, gs, :], over(LEV[:, 0, :], 4), ALU.mult))
                dve.tensor_tensor(R[3][:, gs, :], over(ident, 4), X[0][:, gs, :], ALU.subtract).then_inc(u_ready, 1)
                dve.wait_ge(u_ready, g + 1)
                dve.tensor_tensor(X[0][:, gs, :], R[1][:, gs, :], over(LEV[:, 1, :], 4), ALU.mult).then_inc(b_ready, 1)
                dve.wait_ge(attn_mm, g + 1)
                dve.tensor_tensor(R[0][:, gs, :], bk[g][:, :].rearrange("p (u c) -> p u c", c=P), X[2][:, gs, :],
                                  ALU.mult).then_inc(attn_ready, 1)
            for lv in range(1, NLEV):
                for g in range(4):
                    gs = slice(4 * g, 4 * g + 4)
                    dve.wait_ge(z_mm, 4 * (lv - 1) + g + 1)
                    dve.tensor_tensor(R[3][:, gs, :], R[3][:, gs, :], bk[4 + g][:, :].rearrange("p (u c) -> p u c", c=P),
                                      ALU.subtract).then_inc(u_ready, 1)
                    if lv < NLEV - 1:
                        dve.tensor_tensor(X[0][:, gs, :], R[1][:, gs, :], over(LEV[:, lv + 1, :], 4), ALU.mult
                                          ).then_inc(b_ready, 1)
            state = cbuf[:, 2, 0:HEADS * P].rearrange("p (h d) -> p h d", d=P)
            dve.wait_ge(uw_ready, 8)
            for i in range(NCH):
                t, r0 = i // 2, (i % 2) * CH
                rw = slice(r0, r0 + CH)
                if i > 0:
                    for b in range(2):
                        dve.wait_ge(ws_mm, 2 * (i - 1) + b + 1)
                        v = HSU[rw, t * HEADS + 4 * b:t * HEADS + 4 * b + 4, :]
                        dve.tensor_tensor(v, v, bk[b][rw, :].rearrange("p (u c) -> p u c", c=P), ALU.subtract
                                          ).then_inc(vn_ready, 1)
                if i < NCH - 1:
                    for b in range(2):
                        dve.wait_ge(ks_mm, 2 * i + b + 1)
                        if i > 0:
                            dve.wait_ge(o_mm, 2 * i + b + 1)
                        src = bk[4 + 2 * (i % 2) + b]
                        for hh in range(4 * b, 4 * b + 4):
                            c0 = (hh % 4) * P
                            if i == 0:
                                last = dve.tensor_copy(state[:, hh, :], src[:, c0:c0 + P])
                            else:
                                last = dve.scalar_tensor_tensor(
                                    out=state[:, hh, :], in0=state[:, hh, :],
                                    scalar=X[1][:, t * HEADS + hh, r0 + CH - 1:r0 + CH], in1=src[:, c0:c0 + P],
                                    op0=ALU.mult, op1=ALU.add)
                        last.then_inc(st_ready, 1)
                        dve.wait_ge(st_ready, 2 * i + b + 1)
            ro = sm(200, UN)
            for t in range(TT):
                us = slice(t * HEADS, (t + 1) * HEADS)
                dve.wait_ge(o_raw, 2 * t + 2)
                then(dve.tensor_reduce(ro[:, us], X[3][:, us, :], AX, ALU.add))
                power(ro[:, us], P * EPS)
                for b in range(2):
                    for u in range(t * HEADS + 4 * b, t * HEADS + 4 * b + 4):
                        last = dve.tensor_scalar(X[0][:, u, :], X[0][:, u, :], ro[:, u:u + 1], float(P) ** 0.5,
                                                 ALU.mult, ALU.mult)
                    last.then_inc(o_norm, 1)
            for t in range(TT):
                for b in range(2):
                    dve.wait_ge(o_tp, 2 * t + b + 1)
                    dve.scalar_tensor_tensor(
                        out=HNT[:, 4 * b:4 * b + 4, t * P:(t + 1) * P],
                        in0=bk[4 + 2 * t + b][:, :].rearrange("p (u c) -> p u c", c=P), scalar=gcol[:, G_ON:G_ON + 1],
                        in1=ZT[:, 4 * b:4 * b + 4, t * P:(t + 1) * P], op0=ALU.mult, op1=ALU.mult
                    ).then_inc(og_ready, 1)
            for n in range(2):
                for t in range(TT):
                    dve.wait_ge(wo_mm, 2 * n + t + 1)
                    last = add_to_h(2 * t + n, t, n)
            then(last)
            norm_in(1)
            norm_out(1)
            for f in range(4 * NSL):
                j, i = f // 4, f % 4
                dve.wait_ge(sg_ready, f + 1)
                if j >= 2:
                    dve.wait_ge(d_mm, j - 1)
                dve.tensor_tensor(DHT[:, j % 2, i, :], DSG[:, f % 4, :], bk[4 + i][:, S:2 * S], ALU.mult
                                  ).then_inc(ht_ready, 1)
            dve.wait_ge(d_mm, NSL)
            for t in range(TT):
                for n in range(2):
                    last = add_to_h(2 * t + n, t, n)
            then(last)
            norm_in(2)
            dve.wait_ge(tb_mm, 1)
            dve.tensor_copy(fstage[:, :], bk[4][0:SW_HEADS, 0:FL]).then_inc(tb_ready, 1)
            norm_out(2)
            rk, rq = sm(0, TT * SW_KV), sm(8, TT * SW_HEADS)
            dve.wait_ge(kvq_raw, 2)
            then(dve.tensor_reduce(rk, KSQ.rearrange("p t (g d) -> p (t g) d", d=HD), AX, ALU.add))
            power(rk, HD * EPS)
            then(dve.tensor_scalar(rk, rk, float(HD) ** 0.5, None, ALU.mult))
            for t in range(TT):
                for dup in range(2):
                    last = dve.tensor_tensor(
                        KD[:, t, :, dup * HD:(dup + 1) * HD], KVT[:, t, 0:KVW].rearrange("p (g d) -> p g d", d=HD),
                        bc(rk[:, t * SW_KV:(t + 1) * SW_KV], HD), ALU.mult)
            last.then_inc(k_scaled, 1)
            dve.wait_ge(kvq_raw, 6)
            then(dve.tensor_reduce(rq, QSQ.rearrange("p t (g d) -> p (t g) d", d=HD), AX, ALU.add))
            power(rq, HD * EPS)
            for t in range(TT):
                qv = QTOK[:, t, :].rearrange("p (g d) -> p g d", d=HD)
                last = dve.tensor_tensor(qv, qv, bc(rq[:, t * SW_HEADS:(t + 1) * SW_HEADS], HD), ALU.mult)
            last.then_inc(q_scaled, 1)
            for b in range(4):
                dve.wait_ge(qt_tp, b + 1)
                dve.tensor_scalar(blocks(QT[:, 2 * b:2 * b + 2, :])[:, :, ::-1], blocks(bk[b][:, :]),
                                  gcol[:, G_Q:G_Q + 1], None, ALU.mult).then_inc(qt_ready, 1)
            dve.wait_ge(bias_in, 64)

            def soft_in(b):
                n, hb = b // 2, b % 2
                kw, k0 = (n + 1) * P, (1 - n) * P
                dve.wait_ge(sc_mm, b + 1)
                if b >= 2:
                    dve.wait_ge(pt_tp, PT_FILLS[b - 1])
                for q in range(4):
                    src = bk[q][:, :].rearrange("p (a k) -> p a k", k=S)[:, :, 0:kw]
                    last = dve.tensor_tensor(PR[b % 2][:, 2 * q:2 * q + 2, 0:kw], src,
                                             BIAS[:, 8 * hb + 2 * q:8 * hb + 2 * q + 2, k0:k0 + kw], ALU.add)
                last.then_inc(sc_ready, 1)
                dve.wait_ge(sc_ready, b + 1)
                if b >= 1:
                    dve.wait_ge(ex_ready, b)
                sk = sinkb.rearrange("p (hb cc par) -> p hb par cc", hb=2, par=2)[:, hb]
                then(dve.tensor_reduce(sm(80, 8), PR[b % 2][:, :, 0:kw], AX, ALU.max))
                mx = sm(80, 8).rearrange("p (a c) -> p a c", c=4)
                then(dve.tensor_tensor(mx, mx, sk, ALU.max))
                then(dve.tensor_tensor(sm(88, 8).rearrange("p (a c) -> p a c", c=4), sk, mx, ALU.subtract))
                dve.tensor_scalar(sm(80, 8), sm(80, 8), -1.0, None, ALU.mult).then_inc(mx_ready, 1)

            def soft_out(b):
                n, hb = b // 2, b % 2
                dve.wait_ge(ex_ready, b + 1)
                den = sm(128 + 8 * (b % 2), 8)
                then(dve.tensor_tensor(den, sm(96 + 8 * (b % 2), 8), sm(112 + 8 * (b % 2), 8), ALU.add))
                then(dve.reciprocal(den, den))
                dve.wait_ge(av_mm, b + 1)
                o = OTOK[:, n, :].rearrange("p (hb cc par d) -> p hb par cc d", hb=2, par=2, d=HD)[:, hb]
                for par in range(2):
                    last = dve.tensor_tensor(
                        o[:, par], bk[6][:, par * FS // 2:(par + 1) * FS // 2].rearrange("p (c d) -> p c d", d=HD),
                        bc(den[:, 4 * par:4 * par + 4], HD), ALU.mult)
                last.then_inc(av_ready, 1)

            soft_in(0)
            for b in range(1, 4):
                soft_in(b)
                soft_out(b - 1)
            soft_out(3)
            for b in (0, 2):
                dve.wait_ge(ot_tp, b + 1)
                dve.tensor_copy(blocks(OT[:, 2 * b:2 * b + 2, :])[:, :, ::-1], blocks(bk[b][:, :])
                                ).then_inc(ot_ready, 1)
            for n in range(2):
                for t in range(TT):
                    dve.wait_ge(ao_mm, 2 * n + t + 1)
                    last = add_to_h(4 + 2 * t + n, t, n)
            then(last)
            norm_in(3)
            norm_out(3)

            dve.wait_ge(rt_mm, 1)
            logits = sm(64, 16).rearrange("p (t e) -> p t e", e=EXPERTS)
            then(dve.tensor_copy(sm(64, 16), bk[0][:, 0:16]))
            top = sm(80, 16).rearrange("p (t e) -> p t e", e=8)
            for t in range(TT):
                last = dve.max(top[:, t, :], logits[:, t, :])
            then(last)
            for t in range(TT):
                last = dve.max_index(idx[:, t, :], top[:, t, :], logits[:, t, :])
            then(last)
            ixf = sm(96, 16).rearrange("p (t e) -> p t e", e=8)
            then(dve.tensor_copy(sm(96, 16), idx[:, :, :].rearrange("p t e -> p (t e)")))
            dve.tensor_tensor(sm(0, 2), top[:, :, 1], top[:, :, 0], ALU.subtract).then_inc(rt_ev, 1)
            hot = sm(112, 32).rearrange("p (j t e) -> p j t e", j=2, t=TT)
            for j in range(2):
                for t in range(TT):
                    last = dve.tensor_scalar(hot[:, j, t, :], C("iota8"), ixf[:, t, j:j + 1], None, ALU.is_equal)
            then(last)
            dve.tensor_tensor(MASK, hot[:, 0], hot[:, 1], ALU.add).then_inc(mask_ready, 1)
            dve.wait_ge(rt_ea, 1)
            then(dve.tensor_scalar(sm(4, 2), sm(2, 2), 1.0, None, ALU.add))
            then(dve.reciprocal(sm(4, 2), sm(4, 2)))
            then(dve.tensor_tensor(sm(6, 2), sm(4, 2), sm(2, 2), ALU.mult))
            for t in range(TT):
                last = dve.tensor_scalar(GATE[:, t, 0:EXPERTS], hot[:, 0, t, :], sm(4 + t, 1), None, ALU.mult)
            then(last)
            for t in range(TT):
                last = dve.scalar_tensor_tensor(out=GATE[:, t, 0:EXPERTS], in0=hot[:, 1, t, :], scalar=sm(6 + t, 1),
                                                in1=GATE[:, t, 0:EXPERTS], op0=ALU.mult, op1=ALU.add)
            then(last)
            dve.wait_ge(pos_mm, 1)
            pos = sm(144, 16).rearrange("p (t e) -> p t e", e=EXPERTS)
            dve.reduce_max(sm(8, 1), bk[1][:, 16:24], AX)
            then(dve.tensor_scalar(sm(144, 16), bk[1][:, 0:16], 1.0, None, ALU.add))
            dve.tensor_copy(flag[0:1, 0:1], small[0:1, 8:9])
            then(dve.tensor_tensor(pos, pos, MASK, ALU.mult))
            then(dve.tensor_scalar(sm(144, 16), sm(144, 16), -1.0, None, ALU.add))
            base = C("iota_item").rearrange("p (w e) -> p w e", e=EXPERTS)
            dve.memset(POS[:, :, ITEMS:ITEMS + 1], -1.0)
            dve.memset(GATE[:, :, ITEMS:ITEMS + 1], 0.0)
            for t in range(TT):
                for w in range(NWIN):
                    last = dve.tensor_tensor(POS[:, t, w * EXPERTS:(w + 1) * EXPERTS], pos[:, t, :], base[:, w, :],
                                             ALU.subtract)
                    if w:
                        last = dve.tensor_copy(GATE[:, t, w * EXPERTS:(w + 1) * EXPERTS], GATE[:, t, 0:EXPERTS])
            last.then_inc(flag_ready, 1)
            dve.wait_ge(flag_ready, 1)

            def pick(item):
                for t in range(TT):
                    dve.tensor_scalar(PICK[:, t, :], C("iota_win"), POS[:, t, bass.ds(item, 1)], None, ALU.is_equal)
                    last = dve.tensor_scalar(PICKW[:, t, :], C("iota_win"), POS[:, t, bass.ds(item, 1)],
                                             GATE[:, t, bass.ds(item, 1)], ALU.is_equal, ALU.mult)
                last.then_inc(m_pick, 1)

            def gathered(item):
                for q in range(2):
                    dve.wait_ge(m_gx, 2 * item + q + 1)
                    dve.tensor_tensor(XT[:, 4 * q:4 * q + 4, :],
                                      bk[6 + q][:, 0:4 * WIN].rearrange("p (c s) -> p c s", s=WIN),
                                      bc(gcol[:, GA_FF1 + 4 * q:GA_FF1 + 4 * q + 4], WIN), ALU.mult).then_inc(m_x, 1)

            def expert(item):
                for f in range(2 * NSL):
                    j, b = f // 2, f % 2
                    dve.wait_ge(m_sg, 2 * NSL * item + f + 1)
                    if j >= 2:
                        dve.wait_ge(m_d, NSL * item + j - 1)
                    up = bk[2 + f % 2][:, 0:4 * WIN].rearrange("p (i q s) -> p i q s", i=2, q=2)[:, :, 1, :]
                    dve.tensor_tensor(MHT[:, j % 2, 2 * b:2 * b + 2, :], MSG[:, f % 2, :, :], up, ALU.mult
                                      ).then_inc(m_ht, 1)
                    if f == 2:
                        dve.wait_ge(m_pt, item + 1)
                        pick(item + 1)
                dve.wait_ge(m_gu, 2 * NSL * item + 2 * NSL)
                gathered(item + 1)
                for t in range(TT):
                    for n in range(2):
                        dve.wait_ge(m_y, 4 * item + 2 * t + n + 1)
                        add_to_h((4, 1)[n], t, n).then_inc(m_h, 1)

            pick(0)
            gathered(0)
            expert(0)
            with dve.Fori(1, EXPERTS) as e:
                expert(e)
            more = dve.value_load(flag[0:1, 0:1], min_val=0, max_val=S)
            with dve.If(more > WIN):
                with dve.Fori(EXPERTS, ITEMS) as e:
                    expert(e)


_INS = ["x", "a_norm", "a_w_in", "a_conv", "a_log_decay", "a_dt_bias", "a_out_norm", "a_w_out", "kv_norm", "kv_w",
        "k_norm", "b_norm", "b_w_q", "q_norm", "b_sinks", "b_w_o", "rel_bias", "ffn_norm", "dense_w_gate",
        "dense_w_up", "dense_w_down", "moe_router", "moe_w_gate", "moe_w_up", "moe_w_down"]


def kernel(**inputs):
    import numpy as _np
    import concourse.bacc as _bacc
    from concourse import mybir as _mybir
    from concourse.bass_utils import run_bass_kernel_spmd as _run

    nc = _bacc.Bacc("TRN2", target_bir_lowering=False, num_devices=1)
    main, at, levels, table = constants()
    arrays = {f"in_{n}": _np.ascontiguousarray(inputs[n]) for n in _INS}
    arrays.update(c_main=main, c_levels=levels, c_table=table)
    args = [nc.dram_tensor(n, a.shape, _mybir.dt.from_np(a.dtype), kind="ExternalInput").ap()
            for n, a in arrays.items()]
    out = nc.dram_tensor("out_dram", (1, S, D), _mybir.dt.float32, kind="ExternalOutput").ap()
    build(nc, *args, out, at)
    r = _run(nc, [arrays], core_ids=[0])
    return r.results[0]["out_dram"]
```

```python
from contextlib import ExitStack

import concourse.bass as bass
from concourse import mybir
import numpy as np

F32 = mybir.dt.float32
F32R = mybir.dt.float32r
I32 = mybir.dt.int32
U32 = mybir.dt.uint32
ALU = mybir.AluOpType
ACT = mybir.ActivationFunctionType
AX = mybir.AxisListType.X

P = 128
D = 1024
KT = D // P
S = 256
TT = S // P
HEADS = 8
QKV = 3 * D
CH = 64
NCH = S // CH
UN = TT * HEADS
SW_HEADS, SW_KV, HD = 16, 4, 64
FF = 3584
FS = 512
NSL = FF // FS
EXPERTS = 8
WIN = 128
NWIN = -(-S // WIN)
ITEMS = NWIN * EXPERTS
SLOTS = 7
UNITS = 3 * NSL
HALVES = 2 * UNITS
NHB = 6
AHEAD = NHB - 1
EPS = 1e-6
NEG = -1e30
N_BUCKETS, MAX_DIST = 32, 128
FL = 384

U_IN, U_OUT, U_FF = 0, 8, 10
U_KV = U_FF + 3 * NSL
U_Q, U_O = U_KV + 1, U_KV + 3
U_MOE = U_KV + 5


def g_unit(j):
    return 0 if j == 0 else 3 * j - 1


def d_unit(j):
    return 3 * j + 4 if j < NSL - 1 else 3 * NSL - 1


def ffn_sequence():
    seq = {}
    for j in range(NSL):
        seq[g_unit(j)] = ("gate", j)
        seq[g_unit(j) + 1] = ("up", j)
        seq[d_unit(j)] = ("down", j)
    return [seq[i] for i in range(3 * NSL)]


def constants():
    i = np.arange(P)
    same = (i[:, None] // CH) == (i[None, :] // CH)
    c = {
        "ident": np.eye(P),
        "ones": np.ones((P, P)),
        "up_incl": (i[:, None] <= i[None, :]) & same,
        "same_chunk": same,
        "before": i[:, None] < i[None, :],
        "iota_win": np.tile(np.arange(WIN), (P, 1)),
        "iota_item": np.tile(np.arange(ITEMS) // EXPERTS * WIN, (P, 1)),
        "neg_half": np.full((P, 32), -0.5),
        "iota8": np.tile(np.arange(EXPERTS), (P, 1)),
    }
    main = np.concatenate([np.asarray(v, np.float32) for v in c.values()], axis=1)
    at, off = {}, 0
    for k, v in c.items():
        at[k] = (off, off + v.shape[1])
        off += v.shape[1]
    levels = []
    b = 1
    while b < CH:
        s, t = i[:, None], i[None, :]
        levels.append((s // (2 * b) == t // (2 * b)) & (s // b % 2 == 0) & (t // b % 2 == 1))
        b *= 2
    levels = np.concatenate(levels, axis=1).astype(np.float32)
    dist = 2 * P - 1 - np.arange(FL)
    n = np.maximum(dist, 0)
    exact = N_BUCKETS // 2
    large = exact + (np.log(np.maximum(n, 1).astype(np.float32) / exact) / np.log(MAX_DIST / exact)
                     * (N_BUCKETS - exact)).astype(np.int32)
    bucket = np.where(n < exact, n, np.minimum(large, N_BUCKETS - 1))
    ok = (dist >= 0) & (dist < P)
    table = np.zeros((N_BUCKETS + 1, FL), np.float32)
    for col in range(FL):
        if ok[col]:
            table[bucket[col], col] = 1.0
        else:
            table[N_BUCKETS, col] = NEG
    return main, at, levels, table


def build(nc, x, a_norm, a_w_in, a_conv, a_log_decay, a_dt_bias, a_out_norm, a_w_out, kv_norm, kv_w,
          k_norm, b_norm, b_w_q, q_norm, b_sinks, b_w_o, rel_bias, ffn_norm, dense_w_gate,
          dense_w_up, dense_w_down, moe_router, moe_w_gate, moe_w_up, moe_w_down, c_main, c_levels,
          c_table, out, at):
    NC_MAIN = c_main.shape[1]
    NLEV = c_levels.shape[1] // P
    with ExitStack() as ctx:
        def sb(name, shape, dt=F32):
            return ctx.enter_context(nc.sbuf_tensor(name, shape, dt))

        def sem(name):
            return ctx.enter_context(nc.semaphore(name))

        ring_at = -(-nc.sbuf_base // 64) * 64
        ring = sb("ring", [P, SLOTS, KT, FS])
        h = sb("h", [P, TT, D])
        BS = TT * D
        hs = sb("hs", [P, BS])
        hnT = sb("hnT", [P, BS])
        cbuf = sb("cbuf", [P, 3, BS])
        zbuf = sb("zbuf", [P, BS])
        xbuf = sb("xbuf", [P, 4, BS])
        ring_r = [nc.alloc_sbuf_tensor_at(f"ring_r{i}", [P, 2 * BS], F32R, offset=ring_at + 8 * BS * i)
                  for i in range(SLOTS)]
        bufs_r = [nc.alloc_sbuf_tensor_at(f"buf_r{i}", [P, BS], F32R, offset=ring_at + 8 * BS * SLOTS + 4 * BS * (1 + i))
                  for i in range(10)]
        HS_R, HNT_R, CBUF_R, ZBUF_R, XBUF_R = 0, 1, 2, 5, 6
        cst = sb("cst", [P, NC_MAIN])
        gcol = sb("gcol", [P, 43])
        cw = sb("cw", [P, 96])
        small = sb("small", [P, 344 + 2 * TT * ITEMS])
        bcv = sb("bcv", [P, 32])
        idx = sb("idx", [P, TT, 8], U32)
        flag = sb("flag", [1, 8], I32)
        fstage = sb("fstage", [SW_HEADS, FL])

        bk = [ctx.enter_context(nc.psum_tensor(f"bank{i}", [P, 512], F32)) for i in range(8)]
        bias_dram = nc.dram_tensor("bias_table", (SW_HEADS, FL), F32, kind="Internal")

        def C(name, rows=P):
            a, b = at[name]
            return cst[0:rows, a:b]

        ident, ones = C("ident"), C("ones")

        def as_units(ap):
            return ap.rearrange("p (u d) -> p u d", d=P)

        def blocks(ap):
            if len(ap.shape) == 3:
                return ap.rearrange("p k (n t) -> p (k n) t", t=P)
            return ap.rearrange("p (n t) -> p n t", t=P)

        def as_kt(ap):
            return ap.rearrange("p (k t) -> p k t", t=S)

        HNT = as_kt(hnT[:, :])
        HS = hs[:, :].rearrange("p (t d) -> p t d", d=D)
        CONV = cbuf[:, :, :].rearrange("p b (m t) -> p (b m) t", t=S)
        ZT = as_kt(zbuf[:, :])
        R = [as_units(ring[:, 3 + i // 2, 4 * (i % 2):4 * (i % 2) + 4, :].rearrange("p k f -> p (k f)"))
             for i in range(8)]
        X = [as_units(xbuf[:, i, :]) for i in range(4)]
        CB = [as_units(cbuf[:, i, :]) for i in range(3)]
        HSU = as_units(hs[:, :])
        LEV = hnT[:, 0:NLEV * P].rearrange("p (l c) -> p l c", c=P)
        rows1 = hs[0:96, 0:P]
        rows2 = hs[0:43, P:2 * P]
        wba = xbuf[:, 3, 0:KT * 16].rearrange("p (k n) -> p k n", n=16)
        dtb, alog, sinkb = bcv[:, 0:8], bcv[:, 8:16], bcv[:, 16:32]

        def sm(a, n):
            return small[:, a:a + n]

        DHT = cbuf[:, 0, :].rearrange("p (b i t) -> p b i t", b=2, i=4)
        DSG = cbuf[:, 1, 0:4 * S].rearrange("p (b t) -> p b t", b=4)
        KVW = SW_KV * HD
        RBW = xbuf[0:N_BUCKETS + 1, 2, 0:SW_HEADS]
        RBT = xbuf[0:N_BUCKETS + 1, 2, SW_HEADS:SW_HEADS + FL]
        KVNT = as_kt(xbuf[:, 2, :])
        KVT = zbuf[:, 0:D].rearrange("p (t n) -> p t n", t=TT)
        KD = zbuf[:, D:2 * D].rearrange("p (t g d) -> p t g d", t=TT, g=SW_KV)
        KTD = hnT[:, 0:SW_KV * S].rearrange("p (g t) -> p g t", t=S)
        KSQ = cbuf[:, 2, 0:TT * KVW].rearrange("p (t n) -> p t n", t=TT)
        QSQ = cbuf[:, 0, :].rearrange("p (t n) -> p t n", t=TT)
        QTOK = xbuf[:, 3, :].rearrange("p (t n) -> p t n", t=TT)
        QT = as_kt(cbuf[:, 1, :])
        PR = [cbuf[:, b, :].rearrange("p (a k) -> p a k", a=8) for b in (2, 0)]
        PTR = hs[:, :].rearrange("p (b a q) -> p b a q", b=2, a=8)
        BIAS = xbuf[:, 0:2, :].rearrange("p b (a k) -> p (b a) k", k=S)
        OTOK = xbuf[:, 2, :].rearrange("p (t n) -> p t n", t=TT)
        OT = as_kt(xbuf[:, 3, :])
        PT_FILLS = [0, 2, 4, 8, 12]
        ROUTER = small[:, 280:344].rearrange("p (k n) -> p k n", n=EXPERTS)
        MASK = sm(160, 16).rearrange("p (t e) -> p t e", e=EXPERTS)
        POS, GATE = (small[:, 344 + i * TT * ITEMS:344 + (i + 1) * TT * ITEMS].rearrange("p (t e) -> p t e", t=TT)
                     for i in range(2))
        XF = xbuf[:, 0, KT * WIN:2 * KT * WIN].rearrange("p (k s) -> p k s", s=WIN)
        XH, XL = (bufs_r[XBUF_R][:, i * KT * WIN:(i + 1) * KT * WIN].rearrange("p (k s) -> p k s", s=WIN)
                  for i in range(2))
        MHT = bufs_r[XBUF_R + 1][:, 0:16 * WIN].rearrange("p (b z i s) -> p b z i s", b=2, z=2, i=4)
        MSG, MPR = xbuf[:, 2, 0:FS], xbuf[:, 2, FS:2 * FS]
        OE = xbuf[:, 2, 0:D]
        PICK, PICKW = (xbuf[:, 2, D + i * TT * WIN:D + (i + 1) * TT * WIN].rearrange("p (t s) -> p t s", t=TT)
                       for i in range(2))
        PICKT = xbuf[:, 2, D + 2 * TT * WIN:D + 2 * TT * WIN + S]
        HB = [bufs_r[i][:, :] for i in (CBUF_R, CBUF_R + 1, CBUF_R + 2, HNT_R, ZBUF_R, XBUF_R + 3)]

        GA_FF0, GA_FF1, GA_KV, GA_B = 8, 16, 24, 32
        G_ON, G_Q, G_K = 40, 41, 42
        NORMS = [[(HNT, 0)], [(HNT, GA_FF0)], [(KVNT, GA_KV), (HNT, GA_B)], [(HNT, GA_FF1)]]

        cst_in, par_in, x_in, ba_in, lev_in = (sem(n) for n in ("cst_in", "par_in", "x_in", "ba_in", "lev_in"))
        slot_full = [sem(f"slot_full{i}") for i in range(SLOTS)]
        pow_in, pow_out = sem("pow_in"), sem("pow_out")
        v_seq, a_seq = sem("v_seq"), sem("a_seq")
        par_t, gcol_ready = sem("par_t"), sem("gcol_ready")
        hs_ready, tp_ready, hn_ready = sem("hs_ready"), sem("tp_ready"), sem("hn_ready")
        ba_ready, gate_v, gate_a, cum_ready, gb_ready, egb_ready, dt_ready = (
            sem(n) for n in ("ba_ready", "gate_v", "gate_a", "cum_ready", "gb_ready", "egb_ready", "dt_ready"))
        proj_mm, conv_done, silu_done, z_done = (sem(n) for n in ("proj_mm", "conv_done", "silu_done", "z_done"))
        tok_tp, tok_a, tok_v, scaled = (sem(n) for n in ("tok_tp", "tok_a", "tok_v", "scaled"))
        back_tp, back_a, back_v = (sem(n) for n in ("back_tp", "back_a", "back_v"))
        at_mm, at_ready, attn_mm, attn_ready = (sem(n) for n in ("at_mm", "at_ready", "attn_mm", "attn_ready"))
        b_ready, u_ready, t_tp, t_ready, y_mm, y_ready, z_mm = (
            sem(n) for n in ("b_ready", "u_ready", "t_tp", "t_ready", "y_mm", "y_ready", "z_mm"))
        uw_mm, uw_ready = sem("uw_mm"), sem("uw_ready")
        ws_mm, vn_ready, ks_mm, st_ready, o_mm, o_raw, o_norm, o_tp, og_ready = (
            sem(n) for n in ("ws_mm", "vn_ready", "ks_mm", "st_ready", "o_mm", "o_raw", "o_norm", "o_tp", "og_ready"))
        wo_mm, gu_mm, sg_ready, ht_ready, d_mm = (sem(n) for n in ("wo_mm", "gu_mm", "sg_ready", "ht_ready", "d_mm"))
        rb_one = sem("rb_one")
        rb_in, tb_mm, tb_ready, tb_out, bias_in = (sem(n) for n in ("rb_in", "tb_mm", "tb_ready", "tb_out", "bias_in"))
        kv_mm, q_mm, kvq_raw, k_scaled, q_scaled, kt_tp, kt_ready, qt_tp, qt_ready = (
            sem(n) for n in ("kv_mm", "q_mm", "kvq_raw", "k_scaled", "q_scaled", "kt_tp", "kt_ready", "qt_tp", "qt_ready"))
        sc_mm, sc_ready, mx_ready, ex_ready, pt_tp, pt_ready, av_mm, av_ready = (
            sem(n) for n in ("sc_mm", "sc_ready", "mx_ready", "ex_ready", "pt_tp", "pt_ready", "av_mm", "av_ready"))
        ot_tp, ot_ready, ao_mm = sem("ot_tp"), sem("ot_ready"), sem("ao_mm")
        rt_in, rt_mm, rt_ev, rt_ea, mask_ready, pos_mm, route_ready, flag_ready = (
            sem(n) for n in ("rt_in", "rt_mm", "rt_ev", "rt_ea", "mask_ready", "pos_mm", "route_ready", "flag_ready"))
        m_pick, m_gx, m_xf, m_xh, m_x, m_pt, m_pte = (
            sem(n) for n in ("m_pick", "m_gx", "m_xf", "m_xh", "m_x", "m_pt", "m_pte"))
        m_wh, m_wl, m_used = sem("m_wh"), sem("m_wl"), sem("m_used")
        m_sg, m_pr, m_tp, m_th, m_ht, m_oe, m_y, m_h = (
            sem(n) for n in ("m_sg", "m_pr", "m_tp", "m_th", "m_ht", "m_oe", "m_y", "m_h"))
        stored = sem("stored")

        def cols(w, n):
            return w.rearrange("(k p) f -> p k f", p=P)[:, :, n * FS:(n + 1) * FS]

        def rows(w, n):
            return w[n * FS:(n + 1) * FS, :].rearrange("(i p) f -> p i f", p=P)

        def static_units():
            u = [("c", cols(a_w_in[0], n)) for n in range(8)]
            u += [("c", cols(a_w_out[0], n)) for n in range(2)]
            w = {"gate": dense_w_gate[0], "up": dense_w_up[0], "down": dense_w_down[0]}
            u += [("r", rows(w[k], j)) if k == "down" else ("c", cols(w[k], j)) for k, j in ffn_sequence()]
            u += [("c", cols(kv_w, 0))]
            u += [("c", cols(b_w_q[0], n)) for n in range(2)]
            u += [("c", cols(b_w_o[0], n)) for n in range(2)]
            return u

        def released(n):
            if n < U_OUT:
                return proj_mm, 2 * (n + 1)
            if n < U_FF:
                return wo_mm, 2 * (n - U_OUT + 1)
            if n < U_KV:
                kind, j = ffn_sequence()[n - U_FF]
                return (d_mm, j + 1) if kind == "down" else (gu_mm, 4 * (j + 1))
            if n < U_Q:
                return kv_mm, TT
            if n < U_O:
                return q_mm, TT * (n - U_Q + 1)
            return ao_mm, TT * (n - U_O + 1)

        def slot_c(s):
            return ring[:, s, :, :]

        def slot_r(s):
            return ring[:, s, :, :].rearrange("p k f -> p (k f)").rearrange("p (i f) -> p i f", f=D)

        def landed(eng, n):
            eng.wait_ge(slot_full[n % SLOTS], 16 * (n // SLOTS + 1))

        moe_w = {"gate": moe_w_gate[0], "up": moe_w_up[0], "down": moe_w_down[0]}

        def moe_src(kind, j, e):
            w = moe_w[kind][bass.ds(e, 1)]
            if kind == "down":
                return w[:, j * FS:(j + 1) * FS, :].rearrange("a (i p) f -> p (a i) f", p=P)
            return w.rearrange("a (k p) f -> p (a k) f", p=P)[:, :, j * FS:(j + 1) * FS]

        def moe_landed(eng, item, u):
            n = U_MOE + u
            eng.wait_ge(slot_full[n % SLOTS], 16 * (n // SLOTS + 1) + 16 * (UNITS // SLOTS) * item)

        def half_words(m, base):
            return ring[:, (base + m // 2) % SLOTS, 4 * (m % 2):4 * (m % 2) + 4, :].rearrange("p k f -> p (k f)")

        def half_low(m, base):
            return ring_r[(base + m // 2) % SLOTS][:, (m % 2) * BS:(m % 2 + 1) * BS]

        def g_half(j):
            return 2 * g_unit(j)

        def t_half(j):
            return 6 * j + 5 if j < NSL - 1 else HALVES - 4

        def load(eng, kind, src, s):
            dst = slot_r(s) if kind == "r" else slot_c(s)
            eng.dma_start(dst, src).then_inc(slot_full[s], 16)

        NPAR = 12
        block = ctx.enter_context(nc.Block())

        @block.sync
        def _(sp):
            units = static_units()
            sp.dma_start(h[:, :, :], x[0].rearrange("(t p) d -> p t d", p=P)).then_inc(x_in, 16)
            sp.dma_start(cst[:, :], c_main).then_inc(cst_in, 16)
            for n, (kind, src) in enumerate(units):
                if n >= SLOTS:
                    sp.wait_ge(*released(n - SLOTS))
                if n == U_FF:
                    sp.wait_ge(og_ready, 4)
                load(sp, kind, src, n % SLOTS)
            def expert_item(item, e, first):
                for u, (kind, j) in enumerate(ffn_sequence()):
                    n = U_MOE + u
                    if u < SLOTS and first:
                        sp.wait_ge(*released(n - SLOTS))
                    else:
                        sp.wait_ge(m_used, HALVES * item + 2 * (u - SLOTS + 1))
                    load(sp, "r" if kind == "down" else "c", moe_src(kind, j, e), n % SLOTS)

            expert_item(0, 0, True)
            with sp.Fori(1, EXPERTS) as e:
                expert_item(e, e, False)
            sp.wait_ge(flag_ready, 1)
            more = sp.value_load(flag[0:1, 0:1], min_val=0, max_val=S)
            with sp.If(more > WIN):
                with sp.Fori(1, NWIN) as w:
                    with sp.Fori(0, EXPERTS) as e:
                        expert_item(w * EXPERTS + e, e, False)
                sp.wait_ge(m_h, TT * 2 * ITEMS)
            sp.wait_ge(m_h, TT * 2 * EXPERTS)
            sp.dma_start(out[0].rearrange("(t p) d -> p t d", p=P), h[:, :, :]).then_inc(stored, 16)
            sp.wait_ge(stored, 16)

        @block.gpsimd
        def _(pool):
            pool.dma_start(rows1, a_conv[0].rearrange("j (m p) -> (j m) p", p=P)).then_inc(par_in, 16)
            for r0, src in ((0, a_norm[0]), (GA_FF0, ffn_norm[0]), (GA_FF1, ffn_norm[1]), (GA_KV, kv_norm),
                            (GA_B, b_norm[0])):
                pool.dma_start(rows2[r0:r0 + KT, :], src.rearrange("(m p) -> m p", p=P)).then_inc(par_in, 16)
            pool.dma_start(rows2[G_ON:G_ON + 1, :], a_out_norm).then_inc(par_in, 16)
            for r0, src in ((G_Q, q_norm), (G_K, k_norm.rearrange("(a d) -> a d", a=1))):
                for half in range(2):
                    pool.dma_start(rows2[r0:r0 + 1, half * HD:(half + 1) * HD], src).then_inc(par_in, 16)
            pool.dma_start(bcv[:, 0:8], a_dt_bias[0].partition_broadcast(P)).then_inc(par_in, 16)
            pool.dma_start(bcv[:, 8:16], a_log_decay[0].partition_broadcast(P)).then_inc(ba_in, 16)
            pool.dma_start(bcv[:, 16:32], b_sinks[0].partition_broadcast(P)).then_inc(ba_in, 16)
            pool.dma_start(wba, a_w_in[0].rearrange("(k p) f -> p k f", p=P)[:, :, QKV + D:QKV + D + 16]
                           ).then_inc(ba_in, 16)
            powers = [0]

            def power(ap):
                powers[0] += 1
                pool.wait_ge(pow_in, powers[0])
                pool.tensor_tensor(ap, ap, C("neg_half")[:, 0:ap.shape[1]], ALU.pow).then_inc(pow_out, 1)

            pool.wait_ge(cst_in, 16)
            power(sm(192, TT))
            pool.wait_ge(proj_mm, 16)
            pool.dma_start(hnT[:, 0:NLEV * P], c_levels).then_inc(lev_in, 16)
            power(sm(200, UN))
            power(sm(264, UN))
            for t in range(TT):
                power(sm(200 + t * HEADS, HEADS))
            pool.wait_ge(og_ready, 4)
            pool.memset(xbuf[N_BUCKETS:N_BUCKETS + 1, 2, 0:SW_HEADS], 1.0).then_inc(rb_one, 1)
            pool.dma_start(xbuf[0:N_BUCKETS, 2, 0:SW_HEADS], rel_bias).then_inc(rb_in, 16)
            pool.dma_start(xbuf[0:N_BUCKETS + 1, 2, SW_HEADS:SW_HEADS + FL], c_table).then_inc(rb_in, 16)
            pool.dma_start(ROUTER, moe_router[0].rearrange("(k p) n -> p k n", p=P)).then_inc(rt_in, 16)
            pool.wait_ge(rb_one, 1)
            power(sm(192, TT))
            power(sm(192, TT))
            pool.wait_ge(tb_ready, 1)
            pool.dma_start(bias_dram.ap(), fstage[:, :]).then_inc(tb_out, 16)
            pool.wait_ge(tb_out, 16)
            for g4 in range(4):
                hb, par = g4 // 2, g4 % 2
                src = bass.AP(bias_dram, (8 * hb + par) * FL, [[1, P], [2 * FL, 4], [1, 2 * P]])
                pool.dma_start(BIAS[:, 4 * g4:4 * g4 + 4, :], src).then_inc(bias_in, 16)
            power(sm(0, TT * SW_KV))
            power(sm(8, TT * SW_HEADS))
            power(sm(192, TT))

        @block.tensor
        def _(pe):
            def transpose(o, i, k=P):
                return pe.transpose(o, i, C("ident", k)[:, 0:k])

            def norm(n):
                pe.wait_ge(hs_ready, TT * (n + 1))
                for b in range(4):
                    for c in (2 * b, 2 * b + 1):
                        for t in range(TT):
                            m = transpose(bk[4 + b][:, (c % 2) * S + t * P:(c % 2) * S + (t + 1) * P],
                                          HS[:, t, c * P:(c + 1) * P])
                    m.then_inc(tp_ready, 1)
                pe.wait_ge(hn_ready, 4 * (n + 1))

            pe.wait_ge(cst_in, 16)
            pe.wait_ge(par_in, 16 * NPAR)
            transpose(bk[0][:, 0:96], rows1, 96)
            transpose(bk[0][:, 128:171], rows2, 43).then_inc(par_t, 1)
            norm(0)

            pe.wait_ge(ba_in, 48)
            for t in range(TT):
                for k in range(KT):
                    m = pe.matmul(bk[5][:, 16 * t:16 * t + 16], HNT[:, k, t * P:(t + 1) * P], wba[:, k, :],
                                  start=k == 0, stop=k == KT - 1)
            m.then_inc(ba_ready, 1)

            def project(f):
                u = f // 2
                if f % 2 == 0:
                    landed(pe, U_IN + u)
                if 4 <= f:
                    pe.wait_ge(conv_done, f - 3)
                for q in range(2):
                    c0 = (2 * (f % 2) + q) * P
                    for k in range(KT):
                        m = pe.matmul(bk[f % 4][:, q * S:(q + 1) * S], slot_c(u % SLOTS)[:, k, c0:c0 + P],
                                      HNT[:, k, :], start=k == 0, stop=k == KT - 1)
                m.then_inc(proj_mm, 1)

            for f in range(3):
                project(f)
            pe.wait_ge(gate_v, 2)
            pe.matmul(bk[6][:, 0:UN], C("up_incl"), sm(96, UN), start=True, stop=True)
            pe.matmul(bk[6][:, UN:2 * UN], C("same_chunk"), sm(96, UN), start=True, stop=True).then_inc(cum_ready, 1)
            for f in range(3, 6):
                project(f)
            pe.wait_ge(gate_v, 4)
            for q in range(4):
                pe.matmul(bk[4 + q][:, :], ones, X[0][:, 4 * q:4 * q + 4, :], start=True, stop=True
                          ).then_inc(gb_ready, 1)
            for f in range(6, 16):
                project(f)

            pe.wait_ge(silu_done, 12)
            pe.wait_ge(dt_ready, 4)
            for f in range(12):
                m0, g = (8, 0, 16)[f // 4], f % 4
                if f >= 4:
                    pe.wait_ge(tok_a, f - 3)
                for i in range(4):
                    u = 4 * g + i
                    m = transpose(bk[4 + g][:, i * P:(i + 1) * P],
                                  CONV[:, m0 + u % HEADS, (u // HEADS) * P:(u // HEADS + 1) * P])
                m.then_inc(tok_tp, 1)
            pe.wait_ge(z_done, 4)
            for f in range(12):
                src, g = (R[3], R[4], R[0])[f // 4], f % 4
                if f >= 4:
                    pe.wait_ge(back_a, f - 3)
                pe.wait_ge(scaled, g + 1 if f < 8 else g + 5)
                for i in range(4):
                    m = transpose(bk[g][:, i * P:(i + 1) * P], src[:, 4 * g + i, :])
                m.then_inc(back_tp, 1)
            for g in range(4):
                pe.wait_ge(back_a, 5 + g)
                pe.wait_ge(tok_v, g + 1)
                for u in range(4 * g, 4 * g + 4):
                    m = pe.matmul(bk[4 + g][:, (u % 4) * P:(u % 4 + 1) * P], CB[1][:, u, :], CB[2][:, u, :],
                                  start=True, stop=True)
                m.then_inc(at_mm, 1)
            for g in range(4):
                pe.wait_ge(back_v, g + 1)
                for u in range(4 * g, 4 * g + 4):
                    m = pe.matmul(bk[g][:, (u % 4) * P:(u % 4 + 1) * P], CB[1][:, u, :], CB[0][:, u, :],
                                  start=True, stop=True)
                m.then_inc(attn_mm, 1)

            def turn(lv):
                for g in range(4):
                    pe.wait_ge(u_ready, 4 * lv + g + 1)
                    if lv == 0:
                        pe.wait_ge(attn_ready, g + 1)
                    for u in range(4 * g, 4 * g + 4):
                        m = transpose(bk[g][:, (u % 4) * P:(u % 4 + 1) * P], R[3][:, u, :])
                    m.then_inc(t_tp, 1)

            turn(0)
            for lv in range(1, NLEV):
                for g in range(4):
                    pe.wait_ge(t_ready, 4 * (lv - 1) + g + 1)
                    pe.wait_ge(b_ready, 4 * (lv - 1) + g + 1)
                    for u in range(4 * g, 4 * g + 4):
                        m = pe.matmul(bk[g][:, (u % 4) * P:(u % 4 + 1) * P], X[0][:, u, :], R[4][:, u, :],
                                      start=True, stop=True)
                    m.then_inc(y_mm, 1)
                for g in range(4):
                    pe.wait_ge(y_ready, 4 * (lv - 1) + g + 1)
                    for u in range(4 * g, 4 * g + 4):
                        m = pe.matmul(bk[4 + g][:, (u % 4) * P:(u % 4 + 1) * P], X[3][:, u, :], R[3][:, u, :],
                                      start=True, stop=True)
                    m.then_inc(z_mm, 1)
                if lv < NLEV - 1:
                    turn(lv)
            for g in range(4):
                pe.wait_ge(u_ready, 4 * (NLEV - 1) + g + 1)
                for u in range(4 * g, 4 * g + 4):
                    m = pe.matmul(bk[4 + g][:, (u % 4) * P:(u % 4 + 1) * P], R[3][:, u, :], R[2][:, u, :],
                                  start=True, stop=True)
                m.then_inc(uw_mm, 1)
                for u in range(4 * g, 4 * g + 4):
                    m = pe.matmul(bk[g][:, (u % 4) * P:(u % 4 + 1) * P], R[5][:, u, :], R[3][:, u, :],
                                  start=True, stop=True)
                m.then_inc(uw_mm, 1)
            pe.wait_ge(uw_ready, 8)
            state = cbuf[:, 2, 0:HEADS * P].rearrange("p (h d) -> p h d", d=P)
            for i in range(NCH):
                t, r0 = i // 2, (i % 2) * CH
                rw = slice(r0, r0 + CH)
                if i > 0:
                    for b in range(2):
                        pe.wait_ge(st_ready, 2 * (i - 1) + b + 1)
                        for hh in range(4 * b, 4 * b + 4):
                            m = pe.matmul(bk[b][rw, (hh % 4) * P:(hh % 4 + 1) * P], CB[0][:, t * HEADS + hh, rw],
                                          state[:, hh, :], start=True, stop=True)
                        m.then_inc(ws_mm, 1)
                for b in range(2):
                    if i > 0:
                        pe.wait_ge(vn_ready, 2 * (i - 1) + b + 1)
                    if i == 2:
                        pe.wait_ge(o_raw, b + 1)
                    if i < NCH - 1:
                        for hh in range(4 * b, 4 * b + 4):
                            u = t * HEADS + hh
                            m = pe.matmul(bk[4 + 2 * (i % 2) + b][:, (hh % 4) * P:(hh % 4 + 1) * P],
                                          R[6][rw, u, :], HSU[rw, u, :], start=True, stop=True)
                        m.then_inc(ks_mm, 1)
                    for hh in range(4 * b, 4 * b + 4):
                        u = t * HEADS + hh
                        o = bk[2 + b][rw, (hh % 4) * P:(hh % 4 + 1) * P]
                        if i > 0:
                            pe.matmul(o, R[7][:, u, rw], state[:, hh, :], start=True, stop=False)
                        m = pe.matmul(o, R[0][rw, u, rw], HSU[rw, u, :], start=i == 0, stop=True)
                    m.then_inc(o_mm, 1)
            for t in range(TT):
                for b in range(2):
                    pe.wait_ge(o_norm, 2 * t + b + 1)
                    for hh in range(4 * b, 4 * b + 4):
                        m = transpose(bk[4 + 2 * t + b][:, (hh % 4) * P:(hh % 4 + 1) * P], X[0][:, t * HEADS + hh, :])
                    m.then_inc(o_tp, 1)
            pe.wait_ge(og_ready, 4)
            for n in range(2):
                landed(pe, U_OUT + n)
                for t in range(TT):
                    for k in range(KT):
                        m = pe.matmul(bk[2 * t + n][:, :], HNT[:, k, t * P:(t + 1) * P],
                                      slot_c((U_OUT + n) % SLOTS)[:, k, :], start=k == 0, stop=k == KT - 1)
                    m.then_inc(wo_mm, 1)
            norm(1)

            def gate_up(j):
                landed(pe, U_FF + g_unit(j))
                landed(pe, U_FF + g_unit(j) + 1)
                for i in range(4):
                    if j > 0:
                        pe.wait_ge(ht_ready, 4 * (j - 1) + i + 1)
                    for q in range(2):
                        w = slot_c((U_FF + g_unit(j) + q) % SLOTS)
                        for k in range(KT):
                            m = pe.matmul(bk[4 + i][:, q * S:(q + 1) * S], w[:, k, i * P:(i + 1) * P], HNT[:, k, :],
                                          start=k == 0, stop=k == KT - 1)
                    m.then_inc(gu_mm, 1)

            def down(j):
                landed(pe, U_FF + d_unit(j))
                w = slot_r((U_FF + d_unit(j)) % SLOTS)
                pe.wait_ge(ht_ready, 4 * (j + 1))
                for t in range(TT):
                    for n in range(2):
                        for i in range(4):
                            m = pe.matmul(bk[2 * t + n][:, :], DHT[:, j % 2, i, t * P:(t + 1) * P],
                                          w[:, i, n * FS:(n + 1) * FS], start=j == 0 and i == 0,
                                          stop=j == NSL - 1 and i == 3)
                m.then_inc(d_mm, 1)

            gate_up(0)
            for j in range(1, NSL):
                gate_up(j)
                down(j - 1)
            down(NSL - 1)
            pe.wait_ge(rb_in, 32)
            pe.wait_ge(rb_one, 1)
            pe.matmul(bk[4][0:SW_HEADS, 0:FL], RBW, RBT, start=True, stop=True).then_inc(tb_mm, 1)
            pe.wait_ge(tb_ready, 1)
            norm(2)

            landed(pe, U_KV)
            for t in range(TT):
                for k in range(KT):
                    m = pe.matmul(bk[t][:, :], KVNT[:, k, t * P:(t + 1) * P], slot_c(U_KV % SLOTS)[:, k, :],
                                  start=k == 0, stop=k == KT - 1)
                m.then_inc(kv_mm, 1)
            for n in range(2):
                landed(pe, U_Q + n)
                for t in range(TT):
                    for k in range(KT):
                        m = pe.matmul(bk[2 + 2 * n + t][:, :], HNT[:, k, t * P:(t + 1) * P],
                                      slot_c((U_Q + n) % SLOTS)[:, k, :], start=k == 0, stop=k == KT - 1)
                    m.then_inc(q_mm, 1)
            pe.wait_ge(k_scaled, 1)
            for g in range(SW_KV):
                for t in range(TT):
                    m = transpose(bk[6 + g // 2][:, (g % 2) * S + t * P:(g % 2) * S + (t + 1) * P], KD[:, t, g, :])
                if g % 2:
                    m.then_inc(kt_tp, 1)
            pe.wait_ge(q_scaled, 1)
            for b in range(4):
                for c in (2 * b, 2 * b + 1):
                    for t in range(TT):
                        m = transpose(bk[b][:, (c % 2) * S + t * P:(c % 2) * S + (t + 1) * P],
                                      QTOK[:, t, c * P:(c + 1) * P])
                m.then_inc(qt_tp, 1)
            pe.wait_ge(kt_ready, 2)
            pe.wait_ge(qt_ready, 4)

            def scores(b):
                n, hb = b // 2, b % 2
                k0, kw = (0, P) if n == 0 else (0, 2 * P)
                if b >= 1:
                    pe.wait_ge(sc_ready, b)
                for cc in range(4):
                    for par in range(2):
                        c = 4 * hb + cc
                        rw = slice(par * HD, (par + 1) * HD)
                        m = pe.matmul(bk[2 * par + cc // 2][:, (cc % 2) * S:(cc % 2) * S + kw],
                                      QT[rw, c, n * P:(n + 1) * P], KTD[rw, c // 2, k0:k0 + kw],
                                      start=True, stop=True)
                m.then_inc(sc_mm, 1)

            def weigh(b):
                n, hb = b // 2, b % 2
                nk = n + 1
                pe.wait_ge(ex_ready, b + 1)
                for kb in range(nk):
                    for q in range(2):
                        fills = PT_FILLS[b] + 2 * kb + q
                        if fills >= 2:
                            pe.wait_ge(pt_ready, fills - 1)
                        for a in range(4 * q, 4 * q + 4):
                            m = transpose(bk[4 + q][:, (a % 4) * P:(a % 4 + 1) * P],
                                          PR[b % 2][:, a, kb * P:(kb + 1) * P])
                        m.then_inc(pt_tp, 1)
                pe.wait_ge(pt_ready, PT_FILLS[b + 1])
                if b >= 1:
                    pe.wait_ge(av_ready, b)
                for a in range(8):
                    par, cc = a // 4, a % 4
                    g = (4 * hb + cc) // 2
                    for kb in range(nk):
                        m = pe.matmul(bk[6][:, a * HD:(a + 1) * HD], PTR[:, kb, a, :],
                                      KVT[:, kb, KVW + g * HD:KVW + (g + 1) * HD], start=kb == 0, stop=kb == nk - 1)
                m.then_inc(av_mm, 1)

            scores(0)
            for b in range(1, 4):
                scores(b)
                weigh(b - 1)
            weigh(3)
            pe.wait_ge(av_ready, 4)
            for b in range(4):
                for c in (2 * b, 2 * b + 1):
                    for t in range(TT):
                        m = transpose(bk[b][:, (c % 2) * S + t * P:(c % 2) * S + (t + 1) * P],
                                      OTOK[:, t, c * P:(c + 1) * P])
                m.then_inc(ot_tp, 1)
            pe.wait_ge(ot_ready, 4)
            for n in range(2):
                landed(pe, U_O + n)
                for t in range(TT):
                    for k in range(KT):
                        m = pe.matmul(bk[4 + 2 * t + n][:, :], OT[:, k, t * P:(t + 1) * P],
                                      slot_c((U_O + n) % SLOTS)[:, k, :], start=k == 0, stop=k == KT - 1)
                    m.then_inc(ao_mm, 1)
            norm(3)

            pe.wait_ge(rt_in, 16)
            for t in range(TT):
                for k in range(KT):
                    m = pe.matmul(bk[0][:, 8 * t:8 * t + 8], HNT[:, k, t * P:(t + 1) * P], ROUTER[:, k, :],
                                  start=k == 0, stop=k == KT - 1)
            m.then_inc(rt_mm, 1)
            pe.wait_ge(mask_ready, 1)
            pe.matmul(bk[1][:, 0:8], C("before"), MASK[:, 0, :], start=True, stop=True)
            pe.matmul(bk[1][:, 8:16], ones, MASK[:, 0, :], start=True, stop=False)
            pe.matmul(bk[1][:, 8:16], C("before"), MASK[:, 1, :], start=False, stop=True)
            pe.matmul(bk[1][:, 16:24], ones, MASK[:, 0, :], start=True, stop=False)
            pe.matmul(bk[1][:, 16:24], ones, MASK[:, 1, :], start=False, stop=True).then_inc(pos_mm, 1)

            def gather(item):
                pe.wait_ge(m_pick, item + 1)
                for q in range(2):
                    for c in range(4 * q, 4 * q + 4):
                        for t in range(TT):
                            m = pe.matmul(bk[4 + q][:, (c % 4) * WIN:(c % 4 + 1) * WIN], HS[:, t, c * P:(c + 1) * P],
                                          PICK[:, t, :], start=t == 0, stop=t == TT - 1)
                    m.then_inc(m_gx, 1)

            def gather_pick(item):
                pe.wait_ge(m_pick, item + 1)
                for t in range(TT):
                    m = transpose(bk[7][0:WIN, t * P:(t + 1) * P], PICKW[:, t, :])
                m.then_inc(m_pt, 1)

            def expert(item, first=False, last=False):
                pe.wait_ge(m_x, 2 * item + 2)
                for m in range(HALVES):
                    kind, j = ffn_sequence()[m // 2]
                    pe.wait_ge(m_wl, HALVES * item + m + 1)
                    low = half_low(m, U_MOE)
                    high = HB[m % NHB]
                    if kind == "down":
                        if m % 2 == 0:
                            pe.wait_ge(m_ht, NSL * item + j + 1)
                        if j == 0 and m % 2 == 0 and not first:
                            pe.wait_ge(m_oe, 2 * item)
                        for i2 in range(2):
                            i = 2 * (m % 2) + i2
                            hh, hl = (MHT[:, j % 2, z, i, :] for z in range(2))
                            for n in range(2):
                                c = slice(i2 * D + n * FS, i2 * D + (n + 1) * FS)
                                o = bk[n][0:WIN, :]
                                pe.matmul(o, hh, low[:, c], start=j == 0 and i == 0, stop=False)
                                pe.matmul(o, hl, high[:, c], start=False, stop=False)
                                ins = pe.matmul(o, hh, high[:, c], start=False, stop=j == NSL - 1 and i == 3)
                    else:
                        o = bk[2 + 2 * (j % 2) + (kind == "up")][0:WIN, :]
                        if kind == "gate" and m % 2 == 0:
                            if not (first and j < 2):
                                pe.wait_ge(m_pr, NSL * item + j - 1)
                            if j == 1 and not first:
                                pe.wait_ge(m_h, 4 * item)
                        for k4 in range(4):
                            k = 4 * (m % 2) + k4
                            c = slice(k4 * FS, (k4 + 1) * FS)
                            xh, xl = XH[:, k, :], XL[:, k, :]
                            pe.matmul(o, xh, low[:, c], start=k == 0, stop=False)
                            pe.matmul(o, xl, high[:, c], start=False, stop=False)
                            ins = pe.matmul(o, xh, high[:, c], start=False, stop=k == KT - 1)
                    ins.then_inc(m_used, 1)
                    if m == HALVES - 5 and not last:
                        pe.wait_ge(m_pr, NSL * item + NSL - 1)
                        gather(item + 1)
                    for j in range(NSL):
                        if t_half(j) == m:
                            pe.wait_ge(m_pr, NSL * item + j + 1)
                            if j == 0 and not first:
                                pe.wait_ge(m_h, 4 * item)
                            elif j > 0:
                                pe.wait_ge(m_ht, NSL * item + j)
                            for i in range(4):
                                ins = transpose(bk[6][:, i * WIN:(i + 1) * WIN], MPR[0:WIN, i * P:(i + 1) * P], WIN)
                            ins.then_inc(m_tp, 1)
                pe.wait_ge(m_pte, item + 1)
                for n in range(2):
                    pe.wait_ge(m_oe, 2 * item + n + 1)
                    for t in range(TT):
                        if n == 0 and t == 0:
                            pe.wait_ge(m_ht, NSL * item + NSL)
                        if n == 1 and t == 0 and not last:
                            pe.wait_ge(m_xf, 2 * (item + 1) + 2)
                        pe.matmul(bk[4 + 2 * (1 - n) + t][:, :], PICKT[0:WIN, t * P:(t + 1) * P],
                                  OE[0:WIN, n * FS:(n + 1) * FS], start=True, stop=True).then_inc(m_y, 1)
                if not last:
                    pe.wait_ge(m_h, 4 * item + 2)
                    gather_pick(item + 1)

            gather(0)
            gather_pick(0)
            expert(0, first=True)
            with pe.Fori(1, EXPERTS - 1) as e:
                expert(e)
            expert(EXPERTS - 1, last=True)
            pe.wait_ge(flag_ready, 1)
            more = pe.value_load(flag[0:1, 0:1], min_val=0, max_val=S)
            with pe.If(more > WIN):
                with pe.Fori(EXPERTS, ITEMS) as e:
                    pe.wait_ge(m_h, 4 * e)
                    gather(e)
                    gather_pick(e)
                    expert(e, last=True)

        @block.scalar
        def _(act):
            count = [0]

            def then(ins):
                count[0] += 1
                ins.then_inc(a_seq, 1)
                act.wait_ge(a_seq, count[0])

            def norm(n):
                for b in (1, 3):
                    act.wait_ge(tp_ready, 4 * n + b + 1)
                    for dst, g0 in NORMS[n]:
                        for c in (2 * b, 2 * b + 1):
                            last = act.activation(dst[:, c, :], bk[4 + b][:, (c % 2) * S:(c % 2 + 1) * S], ACT.Copy,
                                                  scale=gcol[:, g0 + c:g0 + c + 1])
                    last.then_inc(hn_ready, 1)

            act.wait_ge(gcol_ready, 1)
            norm(0)
            act.wait_ge(gate_v, 1)
            act.activation(sm(32, UN), sm(0, UN), ACT.Exp)
            act.activation(sm(128, 8), alog, ACT.Exp)
            then(act.activation(sm(48, UN), sm(16, UN), ACT.Exp))
            act.activation(sm(64, UN), sm(48, UN), ACT.Ln, bias=1.0).then_inc(gate_a, 1)
            act.wait_ge(gate_v, 3)
            act.activation(sm(144, UN), sm(112, UN), ACT.Exp)
            act.activation(sm(176, UN), sm(160, UN), ACT.Exp).then_inc(gate_a, 1)
            for q in range(4):
                act.wait_ge(gb_ready, q + 1)
                act.activation(X[1][:, 4 * q:4 * q + 4, :], bk[4 + q][:, :].rearrange("p (u c) -> p u c", c=P),
                               ACT.Exp).then_inc(egb_ready, 1)
            for q in range(4):
                act.wait_ge(dt_ready, q + 1)
                act.activation(X[2][:, 4 * q:4 * q + 4, :], X[2][:, 4 * q:4 * q + 4, :], ACT.Exp
                               ).then_inc(gate_a, 1)
            for f in range(12):
                act.wait_ge(conv_done, f + 1)
                act.activation(CONV[:, 2 * f:2 * f + 2, :], CONV[:, 2 * f:2 * f + 2, :], ACT.Silu
                               ).then_inc(silu_done, 1)
            for f in range(12, 16):
                act.wait_ge(proj_mm, f + 1)
                act.activation(ZT[:, 2 * (f - 12):2 * (f - 12) + 2, :],
                               bk[f % 4][:, :].rearrange("p (m t) -> p m t", t=S), ACT.Silu).then_inc(z_done, 1)
            for f in range(8):
                raw, sq = ((R[1], X[0]), (R[0], X[3]))[f // 4]
                g = f % 4
                act.wait_ge(tok_tp, f + 1)
                src = bk[4 + g][:, :].rearrange("p (u c) -> p u c", c=P)
                act.activation(raw[:, 4 * g:4 * g + 4, :], src, ACT.Copy)
                act.activation(sq[:, 4 * g:4 * g + 4, :], src, ACT.Square).then_inc(tok_a, 1)
            for f in range(8):
                g = f % 4
                act.wait_ge(back_tp, f + 1)
                act.activation(CB[1 + f // 4][:, 4 * g:4 * g + 4, :],
                               bk[g][:, :].rearrange("p (u c) -> p u c", c=P), ACT.Copy).then_inc(back_a, 1)
            for g in range(4):
                act.wait_ge(t_tp, g + 1)
                act.activation(R[4][:, 4 * g:4 * g + 4, :], bk[g][:, :].rearrange("p (u c) -> p u c", c=P),
                               ACT.Copy).then_inc(t_ready, 1)
            for lv in range(1, NLEV):
                for g in range(4):
                    act.wait_ge(y_mm, 4 * (lv - 1) + g + 1)
                    act.activation(X[3][:, 4 * g:4 * g + 4, :], bk[g][:, :].rearrange("p (u c) -> p u c", c=P),
                                   ACT.Copy).then_inc(y_ready, 1)
                if lv < NLEV - 1:
                    for g in range(4):
                        act.wait_ge(t_tp, 4 * lv + g + 1)
                        act.activation(R[4][:, 4 * g:4 * g + 4, :], bk[g][:, :].rearrange("p (u c) -> p u c", c=P),
                                       ACT.Copy).then_inc(t_ready, 1)
            for f in range(8):
                g = f // 2
                act.wait_ge(uw_mm, f + 1)
                dst, b = (HSU, 4 + g) if f % 2 == 0 else (CB[0], g)
                act.activation(dst[:, 4 * g:4 * g + 4, :], bk[b][:, :].rearrange("p (u c) -> p u c", c=P),
                               ACT.Copy).then_inc(uw_ready, 1)
            for t in range(TT):
                for b in range(2):
                    act.wait_ge(o_mm, 4 * t + 2 + b + 1)
                    src = bk[2 + b][:, :].rearrange("p (u c) -> p u c", c=P)
                    u0 = t * HEADS + 4 * b
                    act.activation(X[0][:, u0:u0 + 4, :], src, ACT.Copy)
                    act.activation(X[3][:, u0:u0 + 4, :], src, ACT.Square).then_inc(o_raw, 1)
            norm(1)
            for f in range(4 * NSL):
                act.wait_ge(gu_mm, f + 1)
                if f >= 4:
                    act.wait_ge(ht_ready, f - 3)
                act.activation(DSG[:, f % 4, :], bk[4 + f % 4][:, 0:S], ACT.Silu).then_inc(sg_ready, 1)
            norm(2)
            for t in range(TT):
                act.wait_ge(kv_mm, t + 1)
                act.activation(KVT[:, t, :], bk[t][:, :], ACT.Copy)
                act.activation(KSQ[:, t, :], bk[t][:, 0:KVW], ACT.Square).then_inc(kvq_raw, 1)
            for n in range(2):
                for t in range(TT):
                    act.wait_ge(q_mm, 2 * n + t + 1)
                    b = bk[2 + 2 * n + t]
                    act.activation(QTOK[:, t, n * FS:(n + 1) * FS], b[:, :], ACT.Copy)
                    act.activation(QSQ[:, t, n * FS:(n + 1) * FS], b[:, :], ACT.Square).then_inc(kvq_raw, 1)
            for b in range(2):
                act.wait_ge(kt_tp, b + 1)
                act.activation(KTD[:, 2 * b:2 * b + 2, :], bk[6 + b][:, :].rearrange("p (g t) -> p g t", t=S), ACT.Copy,
                               scale=gcol[:, G_K:G_K + 1]).then_inc(kt_ready, 1)
            for b in range(4):
                n = b // 2
                kw = (n + 1) * P
                act.wait_ge(mx_ready, b + 1)
                for a in range(8):
                    act.activation(PR[b % 2][:, a, 0:kw], PR[b % 2][:, a, 0:kw], ACT.Exp,
                                   bias=sm(80 + a, 1), accum_out=sm(96 + 8 * (b % 2) + a, 1))
                act.activation(sm(112 + 8 * (b % 2), 8), sm(88, 8), ACT.Exp).then_inc(ex_ready, 1)
                for f in range(PT_FILLS[b], PT_FILLS[b + 1]):
                    kb, q = (f - PT_FILLS[b]) // 2, f % 2
                    act.wait_ge(pt_tp, f + 1)
                    if f == PT_FILLS[b] and b >= 1:
                        act.wait_ge(av_mm, b)
                    act.activation(PTR[:, kb, 4 * q:4 * q + 4, :], bk[4 + q][:, :].rearrange("p (u c) -> p u c", c=P),
                                   ACT.Copy).then_inc(pt_ready, 1)
            for b in (1, 3):
                act.wait_ge(ot_tp, b + 1)
                act.activation(blocks(OT[:, 2 * b:2 * b + 2, :])[:, :, ::-1], blocks(bk[b][:, :]),
                               ACT.Copy).then_inc(ot_ready, 1)
            norm(3)
            act.wait_ge(rt_ev, 1)
            act.activation(sm(2, 2), sm(0, 2), ACT.Exp).then_inc(rt_ea, 1)

            def high_x(item):
                for q in range(2):
                    act.wait_ge(m_xf, 2 * item + q + 1)
                    act.activation(XH[:, 4 * q:4 * q + 4, :], XF[:, 4 * q:4 * q + 4, :], ACT.Copy
                                   ).then_inc(m_xh, 1)

            def high_w(item, m, first=False):
                if m % 2 == 0:
                    moe_landed(act, item, m // 2)
                if not (first and m < NHB):
                    act.wait_ge(m_used, HALVES * item + m - NHB + 1)
                act.activation(HB[m % NHB], half_words(m, U_MOE), ACT.Copy).then_inc(m_wh, 1)

            def high_h(item, j):
                act.wait_ge(m_tp, NSL * item + j + 1)
                if j >= 2:
                    act.wait_ge(m_used, HALVES * item + 2 * d_unit(j - 2) + 2)
                act.activation(MHT[:, j % 2, 0, :, :], bk[6][:, 0:4 * WIN].rearrange("p (i s) -> p i s", i=4), ACT.Copy
                               ).then_inc(m_th, 1)

            def pick_t(item, first=False):
                act.wait_ge(m_pt, item + 1)
                if not first:
                    act.wait_ge(m_y, 4 * item)
                act.activation(PICKT[0:WIN, :], bk[7][0:WIN, 0:S], ACT.Copy).then_inc(m_pte, 1)

            def start(item, first=False):
                high_x(item)
                pick_t(item, first)
                for m in range(AHEAD):
                    high_w(item, m, first)

            def expert(item, first=False, last=False):
                for m in range(AHEAD, HALVES + AHEAD):
                    if m < HALVES:
                        high_w(item, m, first)
                    elif not last:
                        high_w(item + 1, m - HALVES)
                    for j in range(NSL):
                        if m == 6 * j + 5:
                            act.wait_ge(m_used, HALVES * item + g_half(j) + 2)
                            if j == 0 and not first:
                                act.wait_ge(m_y, 4 * item)
                            elif j > 0:
                                act.wait_ge(m_pr, NSL * item + j)
                            act.activation(MSG[0:WIN, :], bk[2 + 2 * (j % 2)][0:WIN, :], ACT.Silu).then_inc(m_sg, 1)
                        if m == 6 * j + 9 and j < NSL - 1:
                            high_h(item, j)
                    if m == HALVES + 1 and not last:
                        high_x(item + 1)
                    if m == HALVES + 2:
                        high_h(item, NSL - 1)
                for n in range(2):
                    act.wait_ge(m_used, HALVES * item + HALVES)
                    act.activation(OE[0:WIN, n * FS:(n + 1) * FS], bk[n][0:WIN, :], ACT.Copy).then_inc(m_oe, 1)
                if not last:
                    pick_t(item + 1)

            act.wait_ge(rt_mm, 1)
            start(0, first=True)
            expert(0, first=True)
            with act.Fori(1, EXPERTS - 1) as e:
                expert(e)
            expert(EXPERTS - 1, last=True)
            act.wait_ge(flag_ready, 1)
            more = act.value_load(flag[0:1, 0:1], min_val=0, max_val=S)
            with act.If(more > WIN):
                with act.Fori(EXPERTS, ITEMS) as e:
                    start(e)
                    expert(e, last=True)

        @block.vector
        def _(dve):
            count = [0]
            powers = [0]

            def then(ins):
                count[0] += 1
                ins.then_inc(v_seq, 1)
                dve.wait_ge(v_seq, count[0])

            def bc(ap, n):
                return ap.unsqueeze(2).to_broadcast([P, ap.shape[1], n])

            def over(ap, m):
                return ap.unsqueeze(1).to_broadcast([P, m, ap.shape[1]])

            def power(ap, eps):
                powers[0] += 1
                dve.tensor_scalar(ap, ap, float(eps), None, ALU.add).then_inc(pow_in, 1)
                dve.wait_ge(pow_out, powers[0])

            def norm_in(n):
                for t in range(TT):
                    last = dve.tensor_tensor_reduce(out=HS[:, t, :], in0=h[:, t, :], in1=h[:, t, :], scale=1.0,
                                                    scalar=0.0, op0=ALU.mult, op1=ALU.add,
                                                    accum_out=sm(192 + t, 1))
                then(last)
                power(sm(192, TT), D * EPS)
                for t in range(TT):
                    dve.tensor_scalar(HS[:, t, :], h[:, t, :], sm(192 + t, 1), float(D) ** 0.5, ALU.mult, ALU.mult
                                      ).then_inc(hs_ready, 1)

            def norm_out(n):
                for b in (0, 2):
                    dve.wait_ge(tp_ready, 4 * n + b + 1)
                    for dst, g0 in NORMS[n]:
                        for c in (2 * b, 2 * b + 1):
                            last = dve.tensor_scalar(dst[:, c, :], bk[4 + b][:, (c % 2) * S:(c % 2 + 1) * S],
                                                     gcol[:, g0 + c:g0 + c + 1], None, ALU.mult)
                    last.then_inc(hn_ready, 1)

            def add_to_h(b, t, n):
                hh = h[:, t, n * FS:(n + 1) * FS]
                return dve.tensor_tensor(hh, hh, bk[b][:, :], ALU.add)

            dve.wait_ge(par_t, 1)
            dve.tensor_copy(cw[:, :], bk[0][:, 0:96])
            dve.tensor_copy(gcol[:, :], bk[0][:, 128:171]).then_inc(gcol_ready, 1)
            dve.wait_ge(gcol_ready, 1)
            dve.wait_ge(x_in, 16)
            norm_in(0)
            norm_out(0)
            dve.wait_ge(ba_ready, 1)
            ba = bk[5][:, 0:2 * UN].rearrange("p (t n) -> p t n", n=2 * HEADS)

            def u2(a):
                return sm(a, UN).rearrange("p (t h) -> p t h", h=HEADS)

            dve.tensor_scalar(u2(0), ba[:, :, 0:HEADS], -1.0, None, ALU.mult)
            then(dve.tensor_tensor(u2(80), ba[:, :, HEADS:2 * HEADS], over(dtb, TT), ALU.add))
            then(dve.tensor_scalar(sm(16, UN), sm(80, UN), -1.0, None, ALU.mult))
            dve.tensor_tensor(sm(16, UN), sm(16, UN), sm(80, UN), ALU.min).then_inc(gate_v, 1)
            dve.wait_ge(gate_a, 1)
            dve.tensor_scalar(sm(0, UN), sm(32, UN), 1.0, None, ALU.add)
            then(dve.tensor_scalar(sm(80, UN), sm(80, UN), 0.0, None, ALU.max))
            dve.reciprocal(sm(32, UN), sm(0, UN))
            then(dve.tensor_tensor(sm(80, UN), sm(80, UN), sm(64, UN), ALU.add))
            dve.scalar_tensor_tensor(out=u2(96), in0=u2(80), scalar=-1.0, in1=over(sm(128, 8), TT), op0=ALU.mult,
                                     op1=ALU.mult).then_inc(gate_v, 1)

            def conv(f):
                dve.wait_ge(proj_mm, f + 1)
                b = bk[f % 4]
                for q in range(2):
                    m = 2 * f + q
                    last = dve.tensor_scalar(CONV[:, m, :], b[:, q * S:(q + 1) * S], cw[:, 72 + m:73 + m], None,
                                             ALU.mult)
                for lag in range(1, 4):
                    then(last)
                    for q in range(2):
                        m = 2 * f + q
                        tap = (3 - lag) * 24 + m
                        last = dve.scalar_tensor_tensor(
                            out=CONV[:, m, lag:S], in0=b[:, q * S:(q + 1) * S - lag], scalar=cw[:, tap:tap + 1],
                            in1=CONV[:, m, lag:S], op0=ALU.mult, op1=ALU.add)
                last.then_inc(conv_done, 1)

            conv(0)
            conv(1)
            dve.wait_ge(cum_ready, 1)
            then(dve.tensor_copy(sm(112, UN), bk[6][:, 0:UN]))
            dve.tensor_tensor(sm(160, UN), bk[6][:, UN:2 * UN], sm(112, UN), ALU.subtract).then_inc(gate_v, 1)
            for u in range(UN):
                last = dve.tensor_scalar(X[0][:, u, :], ident, sm(112 + u, 1), None, ALU.mult)
            last.then_inc(gate_v, 1)
            conv(2)
            conv(3)
            for q in range(4):
                dve.wait_ge(egb_ready, q + 1)
                for i in range(4):
                    u = 4 * q + i
                    last = dve.tensor_scalar(X[2][:, u, :], bk[4 + q][:, i * P:(i + 1) * P], sm(112 + u, 1), 0.0,
                                             ALU.subtract, ALU.min)
                last.then_inc(dt_ready, 1)
            for f in range(4, 12):
                conv(f)
            for q in range(4):
                dve.wait_ge(gate_a, 3 + q)
                last = dve.tensor_tensor(X[2][:, 4 * q:4 * q + 4, :], X[2][:, 4 * q:4 * q + 4, :],
                                         over(C("up_incl"), 4), ALU.mult)
            then(last)
            beta, eg, etail = sm(32, UN), sm(144, UN), sm(176, UN)
            rk, rkb, rkbe, rkt, rq = (sm(200 + 16 * i, UN) for i in range(4 + 1))
            for g in range(4):
                dve.wait_ge(tok_a, g + 1)
                last = dve.tensor_reduce(rk[:, 4 * g:4 * g + 4], X[0][:, 4 * g:4 * g + 4, :], AX, ALU.add)
            then(last)
            power(rk, EPS)
            dve.tensor_tensor(rkb, rk, beta, ALU.mult)
            then(dve.tensor_tensor(rkt, rk, etail, ALU.mult))
            then(dve.tensor_tensor(rkbe, rkb, eg, ALU.mult))
            for g in range(4):
                for u in range(4 * g, 4 * g + 4):
                    for dst, r in ((3, rk), (4, rkb), (5, rkbe), (6, rkt)):
                        last = dve.tensor_scalar(R[dst][:, u, :], R[1][:, u, :], r[:, u:u + 1], None, ALU.mult)
                last.then_inc(scaled, 1)
            for g in range(4):
                dve.wait_ge(tok_a, g + 5)
                last = dve.tensor_reduce(rq[:, 4 * g:4 * g + 4], X[3][:, 4 * g:4 * g + 4, :], AX, ALU.add)
            then(last)
            power(rq, EPS)
            for g in range(4):
                for u in range(4 * g, 4 * g + 4):
                    last = dve.tensor_scalar(R[0][:, u, :], R[0][:, u, :], rq[:, u:u + 1], float(P) ** -0.5,
                                             ALU.mult, ALU.mult)
                last.then_inc(scaled, 1)
            for g in range(4):
                dve.wait_ge(tok_tp, 9 + g)
                last = dve.tensor_tensor(R[2][:, 4 * g:4 * g + 4, :], bk[4 + g][:, :].rearrange("p (u c) -> p u c", c=P),
                                         bc(beta[:, 4 * g:4 * g + 4], P), ALU.mult)
                last.then_inc(tok_v, 1)
            for g in range(4):
                dve.wait_ge(back_tp, 9 + g)
                src = bk[g][:, :].rearrange("p (u c) -> p u c", c=P)
                dve.tensor_copy(CB[0][:, 4 * g:4 * g + 4, :], src)
                dve.tensor_tensor(R[7][:, 4 * g:4 * g + 4, :], src, X[1][:, 4 * g:4 * g + 4, :], ALU.mult
                                  ).then_inc(back_v, 1)
            dve.wait_ge(lev_in, 16)
            for g in range(4):
                dve.wait_ge(at_mm, g + 1)
                gs = slice(4 * g, 4 * g + 4)
                then(dve.tensor_tensor(R[1][:, gs, :], bk[4 + g][:, :].rearrange("p (u c) -> p u c", c=P),
                                       X[2][:, gs, :], ALU.mult))
                then(dve.tensor_tensor(X[0][:, gs, :], R[1][:, gs, :], over(LEV[:, 0, :], 4), ALU.mult))
                dve.tensor_tensor(R[3][:, gs, :], over(ident, 4), X[0][:, gs, :], ALU.subtract).then_inc(u_ready, 1)
                dve.wait_ge(u_ready, g + 1)
                dve.tensor_tensor(X[0][:, gs, :], R[1][:, gs, :], over(LEV[:, 1, :], 4), ALU.mult).then_inc(b_ready, 1)
                dve.wait_ge(attn_mm, g + 1)
                dve.tensor_tensor(R[0][:, gs, :], bk[g][:, :].rearrange("p (u c) -> p u c", c=P), X[2][:, gs, :],
                                  ALU.mult).then_inc(attn_ready, 1)
            for lv in range(1, NLEV):
                for g in range(4):
                    gs = slice(4 * g, 4 * g + 4)
                    dve.wait_ge(z_mm, 4 * (lv - 1) + g + 1)
                    dve.tensor_tensor(R[3][:, gs, :], R[3][:, gs, :], bk[4 + g][:, :].rearrange("p (u c) -> p u c", c=P),
                                      ALU.subtract).then_inc(u_ready, 1)
                    if lv < NLEV - 1:
                        dve.tensor_tensor(X[0][:, gs, :], R[1][:, gs, :], over(LEV[:, lv + 1, :], 4), ALU.mult
                                          ).then_inc(b_ready, 1)
            state = cbuf[:, 2, 0:HEADS * P].rearrange("p (h d) -> p h d", d=P)
            dve.wait_ge(uw_ready, 8)
            for i in range(NCH):
                t, r0 = i // 2, (i % 2) * CH
                rw = slice(r0, r0 + CH)
                if i > 0:
                    for b in range(2):
                        dve.wait_ge(ws_mm, 2 * (i - 1) + b + 1)
                        v = HSU[rw, t * HEADS + 4 * b:t * HEADS + 4 * b + 4, :]
                        dve.tensor_tensor(v, v, bk[b][rw, :].rearrange("p (u c) -> p u c", c=P), ALU.subtract
                                          ).then_inc(vn_ready, 1)
                if i < NCH - 1:
                    for b in range(2):
                        dve.wait_ge(ks_mm, 2 * i + b + 1)
                        if i > 0:
                            dve.wait_ge(o_mm, 2 * i + b + 1)
                        src = bk[4 + 2 * (i % 2) + b]
                        for hh in range(4 * b, 4 * b + 4):
                            c0 = (hh % 4) * P
                            if i == 0:
                                last = dve.tensor_copy(state[:, hh, :], src[:, c0:c0 + P])
                            else:
                                last = dve.scalar_tensor_tensor(
                                    out=state[:, hh, :], in0=state[:, hh, :],
                                    scalar=X[1][:, t * HEADS + hh, r0 + CH - 1:r0 + CH], in1=src[:, c0:c0 + P],
                                    op0=ALU.mult, op1=ALU.add)
                        last.then_inc(st_ready, 1)
                        dve.wait_ge(st_ready, 2 * i + b + 1)
            ro = sm(200, UN)
            for t in range(TT):
                us = slice(t * HEADS, (t + 1) * HEADS)
                dve.wait_ge(o_raw, 2 * t + 2)
                then(dve.tensor_reduce(ro[:, us], X[3][:, us, :], AX, ALU.add))
                power(ro[:, us], P * EPS)
                for b in range(2):
                    for u in range(t * HEADS + 4 * b, t * HEADS + 4 * b + 4):
                        last = dve.tensor_scalar(X[0][:, u, :], X[0][:, u, :], ro[:, u:u + 1], float(P) ** 0.5,
                                                 ALU.mult, ALU.mult)
                    last.then_inc(o_norm, 1)
            for t in range(TT):
                for b in range(2):
                    dve.wait_ge(o_tp, 2 * t + b + 1)
                    dve.scalar_tensor_tensor(
                        out=HNT[:, 4 * b:4 * b + 4, t * P:(t + 1) * P],
                        in0=bk[4 + 2 * t + b][:, :].rearrange("p (u c) -> p u c", c=P), scalar=gcol[:, G_ON:G_ON + 1],
                        in1=ZT[:, 4 * b:4 * b + 4, t * P:(t + 1) * P], op0=ALU.mult, op1=ALU.mult
                    ).then_inc(og_ready, 1)
            for n in range(2):
                for t in range(TT):
                    dve.wait_ge(wo_mm, 2 * n + t + 1)
                    last = add_to_h(2 * t + n, t, n)
            then(last)
            norm_in(1)
            norm_out(1)
            for f in range(4 * NSL):
                j, i = f // 4, f % 4
                dve.wait_ge(sg_ready, f + 1)
                if j >= 2:
                    dve.wait_ge(d_mm, j - 1)
                dve.tensor_tensor(DHT[:, j % 2, i, :], DSG[:, f % 4, :], bk[4 + i][:, S:2 * S], ALU.mult
                                  ).then_inc(ht_ready, 1)
            dve.wait_ge(d_mm, NSL)
            for t in range(TT):
                for n in range(2):
                    last = add_to_h(2 * t + n, t, n)
            then(last)
            norm_in(2)
            dve.wait_ge(tb_mm, 1)
            dve.tensor_copy(fstage[:, :], bk[4][0:SW_HEADS, 0:FL]).then_inc(tb_ready, 1)
            norm_out(2)
            rk, rq = sm(0, TT * SW_KV), sm(8, TT * SW_HEADS)
            dve.wait_ge(kvq_raw, 2)
            then(dve.tensor_reduce(rk, KSQ.rearrange("p t (g d) -> p (t g) d", d=HD), AX, ALU.add))
            power(rk, HD * EPS)
            then(dve.tensor_scalar(rk, rk, float(HD) ** 0.5, None, ALU.mult))
            for t in range(TT):
                for dup in range(2):
                    last = dve.tensor_tensor(
                        KD[:, t, :, dup * HD:(dup + 1) * HD], KVT[:, t, 0:KVW].rearrange("p (g d) -> p g d", d=HD),
                        bc(rk[:, t * SW_KV:(t + 1) * SW_KV], HD), ALU.mult)
            last.then_inc(k_scaled, 1)
            dve.wait_ge(kvq_raw, 6)
            then(dve.tensor_reduce(rq, QSQ.rearrange("p t (g d) -> p (t g) d", d=HD), AX, ALU.add))
            power(rq, HD * EPS)
            for t in range(TT):
                qv = QTOK[:, t, :].rearrange("p (g d) -> p g d", d=HD)
                last = dve.tensor_tensor(qv, qv, bc(rq[:, t * SW_HEADS:(t + 1) * SW_HEADS], HD), ALU.mult)
            last.then_inc(q_scaled, 1)
            for b in range(4):
                dve.wait_ge(qt_tp, b + 1)
                dve.tensor_scalar(blocks(QT[:, 2 * b:2 * b + 2, :])[:, :, ::-1], blocks(bk[b][:, :]),
                                  gcol[:, G_Q:G_Q + 1], None, ALU.mult).then_inc(qt_ready, 1)
            dve.wait_ge(bias_in, 64)

            def soft_in(b):
                n, hb = b // 2, b % 2
                kw, k0 = (n + 1) * P, (1 - n) * P
                dve.wait_ge(sc_mm, b + 1)
                if b >= 2:
                    dve.wait_ge(pt_tp, PT_FILLS[b - 1])
                for q in range(4):
                    src = bk[q][:, :].rearrange("p (a k) -> p a k", k=S)[:, :, 0:kw]
                    last = dve.tensor_tensor(PR[b % 2][:, 2 * q:2 * q + 2, 0:kw], src,
                                             BIAS[:, 8 * hb + 2 * q:8 * hb + 2 * q + 2, k0:k0 + kw], ALU.add)
                last.then_inc(sc_ready, 1)
                dve.wait_ge(sc_ready, b + 1)
                if b >= 1:
                    dve.wait_ge(ex_ready, b)
                sk = sinkb.rearrange("p (hb cc par) -> p hb par cc", hb=2, par=2)[:, hb]
                then(dve.tensor_reduce(sm(80, 8), PR[b % 2][:, :, 0:kw], AX, ALU.max))
                mx = sm(80, 8).rearrange("p (a c) -> p a c", c=4)
                then(dve.tensor_tensor(mx, mx, sk, ALU.max))
                then(dve.tensor_tensor(sm(88, 8).rearrange("p (a c) -> p a c", c=4), sk, mx, ALU.subtract))
                dve.tensor_scalar(sm(80, 8), sm(80, 8), -1.0, None, ALU.mult).then_inc(mx_ready, 1)

            def soft_out(b):
                n, hb = b // 2, b % 2
                dve.wait_ge(ex_ready, b + 1)
                den = sm(128 + 8 * (b % 2), 8)
                then(dve.tensor_tensor(den, sm(96 + 8 * (b % 2), 8), sm(112 + 8 * (b % 2), 8), ALU.add))
                then(dve.reciprocal(den, den))
                dve.wait_ge(av_mm, b + 1)
                o = OTOK[:, n, :].rearrange("p (hb cc par d) -> p hb par cc d", hb=2, par=2, d=HD)[:, hb]
                for par in range(2):
                    last = dve.tensor_tensor(
                        o[:, par], bk[6][:, par * FS // 2:(par + 1) * FS // 2].rearrange("p (c d) -> p c d", d=HD),
                        bc(den[:, 4 * par:4 * par + 4], HD), ALU.mult)
                last.then_inc(av_ready, 1)

            soft_in(0)
            for b in range(1, 4):
                soft_in(b)
                soft_out(b - 1)
            soft_out(3)
            for b in (0, 2):
                dve.wait_ge(ot_tp, b + 1)
                dve.tensor_copy(blocks(OT[:, 2 * b:2 * b + 2, :])[:, :, ::-1], blocks(bk[b][:, :])
                                ).then_inc(ot_ready, 1)
            for n in range(2):
                for t in range(TT):
                    dve.wait_ge(ao_mm, 2 * n + t + 1)
                    last = add_to_h(4 + 2 * t + n, t, n)
            then(last)
            norm_in(3)
            norm_out(3)

            dve.wait_ge(rt_mm, 1)
            logits = sm(64, 16).rearrange("p (t e) -> p t e", e=EXPERTS)
            then(dve.tensor_copy(sm(64, 16), bk[0][:, 0:16]))
            top = sm(80, 16).rearrange("p (t e) -> p t e", e=8)
            for t in range(TT):
                last = dve.max(top[:, t, :], logits[:, t, :])
            then(last)
            for t in range(TT):
                last = dve.max_index(idx[:, t, :], top[:, t, :], logits[:, t, :])
            then(last)
            ixf = sm(96, 16).rearrange("p (t e) -> p t e", e=8)
            then(dve.tensor_copy(sm(96, 16), idx[:, :, :].rearrange("p t e -> p (t e)")))
            dve.tensor_tensor(sm(0, 2), top[:, :, 1], top[:, :, 0], ALU.subtract).then_inc(rt_ev, 1)
            hot = sm(112, 32).rearrange("p (j t e) -> p j t e", j=2, t=TT)
            for j in range(2):
                for t in range(TT):
                    last = dve.tensor_scalar(hot[:, j, t, :], C("iota8"), ixf[:, t, j:j + 1], None, ALU.is_equal)
            then(last)
            dve.tensor_tensor(MASK, hot[:, 0], hot[:, 1], ALU.add).then_inc(mask_ready, 1)
            dve.wait_ge(rt_ea, 1)
            then(dve.tensor_scalar(sm(4, 2), sm(2, 2), 1.0, None, ALU.add))
            then(dve.reciprocal(sm(4, 2), sm(4, 2)))
            then(dve.tensor_tensor(sm(6, 2), sm(4, 2), sm(2, 2), ALU.mult))
            for t in range(TT):
                last = dve.tensor_scalar(GATE[:, t, 0:EXPERTS], hot[:, 0, t, :], sm(4 + t, 1), None, ALU.mult)
            then(last)
            for t in range(TT):
                last = dve.scalar_tensor_tensor(out=GATE[:, t, 0:EXPERTS], in0=hot[:, 1, t, :], scalar=sm(6 + t, 1),
                                                in1=GATE[:, t, 0:EXPERTS], op0=ALU.mult, op1=ALU.add)
            then(last)
            dve.wait_ge(pos_mm, 1)
            pos = sm(144, 16).rearrange("p (t e) -> p t e", e=EXPERTS)
            dve.reduce_max(sm(8, 1), bk[1][:, 16:24], AX)
            then(dve.tensor_scalar(sm(144, 16), bk[1][:, 0:16], 1.0, None, ALU.add))
            dve.tensor_copy(flag[0:1, 0:1], small[0:1, 8:9])
            then(dve.tensor_tensor(pos, pos, MASK, ALU.mult))
            then(dve.tensor_scalar(sm(144, 16), sm(144, 16), -1.0, None, ALU.add))
            base = C("iota_item").rearrange("p (w e) -> p w e", e=EXPERTS)
            for t in range(TT):
                for w in range(NWIN):
                    last = dve.tensor_tensor(POS[:, t, w * EXPERTS:(w + 1) * EXPERTS], pos[:, t, :], base[:, w, :],
                                             ALU.subtract)
                    if w:
                        last = dve.tensor_copy(GATE[:, t, w * EXPERTS:(w + 1) * EXPERTS], GATE[:, t, 0:EXPERTS])
            last.then_inc(flag_ready, 1)
            dve.wait_ge(flag_ready, 1)

            def pick(item):
                for t in range(TT):
                    dve.tensor_scalar(PICK[:, t, :], C("iota_win"), POS[:, t, bass.ds(item, 1)], None, ALU.is_equal)
                    last = dve.tensor_scalar(PICKW[:, t, :], C("iota_win"), POS[:, t, bass.ds(item, 1)],
                                             GATE[:, t, bass.ds(item, 1)], ALU.is_equal, ALU.mult)
                last.then_inc(m_pick, 1)

            def gathered(item):
                for q in range(2):
                    dve.wait_ge(m_gx, 2 * item + q + 1)
                    dve.tensor_tensor(XF[:, 4 * q:4 * q + 4, :],
                                      bk[4 + q][:, 0:4 * WIN].rearrange("p (c s) -> p c s", s=WIN),
                                      bc(gcol[:, GA_FF1 + 4 * q:GA_FF1 + 4 * q + 4], WIN), ALU.mult).then_inc(m_xf, 1)

            def low_x(item, q):
                dve.wait_ge(m_xh, 2 * item + q + 1)
                cs = slice(4 * q, 4 * q + 4)
                dve.tensor_tensor(XL[:, cs, :], XF[:, cs, :], XH[:, cs, :], ALU.subtract).then_inc(m_x, 1)

            def low_w(item, m):
                dve.wait_ge(m_wh, HALVES * item + m + 1)
                dve.tensor_tensor(half_low(m, U_MOE), half_words(m, U_MOE), HB[m % NHB], ALU.subtract).then_inc(m_wl, 1)

            def hidden(item, j):
                dve.wait_ge(m_sg, NSL * item + j + 1)
                if j > 0:
                    dve.wait_ge(m_tp, NSL * item + j)
                dve.wait_ge(m_used, HALVES * item + g_half(j) + 4)
                dve.tensor_tensor(MPR[0:WIN, :], MSG[0:WIN, :], bk[3 + 2 * (j % 2)][0:WIN, :], ALU.mult
                                  ).then_inc(m_pr, 1)

            def low_h(item, j):
                dve.wait_ge(m_th, NSL * item + j + 1)
                dve.tensor_tensor(MHT[:, j % 2, 1, :, :], bk[6][:, 0:4 * WIN].rearrange("p (i s) -> p i s", i=4),
                                  MHT[:, j % 2, 0, :, :], ALU.subtract).then_inc(m_ht, 1)

            def start(item):
                pick(item)
                gathered(item)
                for q in range(2):
                    low_x(item, q)
                for m in range(AHEAD):
                    low_w(item, m)

            def expert(item, last=False):
                for m in range(AHEAD, HALVES + AHEAD):
                    if m < HALVES:
                        low_w(item, m)
                    elif not last:
                        low_w(item + 1, m - HALVES)
                    for j in range(NSL):
                        if m == 6 * j + 5:
                            hidden(item, j)
                        if m == 6 * j + 9 and j < NSL - 1:
                            low_h(item, j)
                    if m == HALVES // 2 and not last:
                        dve.wait_ge(m_pt, item + 1)
                        pick(item + 1)
                    if m == HALVES - 1 and not last:
                        gathered(item + 1)
                    if m == HALVES + 1:
                        if not last:
                            for q in range(2):
                                low_x(item + 1, q)
                        low_h(item, NSL - 1)
                for n in range(2):
                    for t in range(TT):
                        dve.wait_ge(m_y, 4 * item + 2 * n + t + 1)
                        add_to_h(4 + 2 * (1 - n) + t, t, n).then_inc(m_h, 1)

            start(0)
            expert(0)
            with dve.Fori(1, EXPERTS - 1) as e:
                expert(e)
            expert(EXPERTS - 1, last=True)
            more = dve.value_load(flag[0:1, 0:1], min_val=0, max_val=S)
            with dve.If(more > WIN):
                with dve.Fori(EXPERTS, ITEMS) as e:
                    start(e)
                    expert(e, last=True)


_INS = ["x", "a_norm", "a_w_in", "a_conv", "a_log_decay", "a_dt_bias", "a_out_norm", "a_w_out", "kv_norm", "kv_w",
        "k_norm", "b_norm", "b_w_q", "q_norm", "b_sinks", "b_w_o", "rel_bias", "ffn_norm", "dense_w_gate",
        "dense_w_up", "dense_w_down", "moe_router", "moe_w_gate", "moe_w_up", "moe_w_down"]


def kernel(**inputs):
    import numpy as _np
    import concourse.bacc as _bacc
    from concourse import mybir as _mybir
    from concourse.bass_utils import run_bass_kernel_spmd as _run

    nc = _bacc.Bacc("TRN2", target_bir_lowering=False, num_devices=1)
    main, at, levels, table = constants()
    arrays = {f"in_{n}": _np.ascontiguousarray(inputs[n]) for n in _INS}
    arrays.update(c_main=main, c_levels=levels, c_table=table)
    args = [nc.dram_tensor(n, a.shape, _mybir.dt.from_np(a.dtype), kind="ExternalInput").ap()
            for n, a in arrays.items()]
    out = nc.dram_tensor("out_dram", (1, S, D), _mybir.dt.float32, kind="ExternalOutput").ap()
    build(nc, *args, out, at)
    r = _run(nc, [arrays], core_ids=[0])
    return r.results[0]["out_dram"]
```
